# Optimizing a Trainium2 kernel written in Bass

```python
import jax, jax.numpy as jnp
from jax import lax
import numpy as np

D_MODEL = 2048
BATCH = 1
SEQ = 256
DEPTH = 1

HEAD_DIM = 128
N_HEADS_TOTAL = D_MODEL // HEAD_DIM
NA_HEADS = N_HEADS_TOTAL // 2
GQA_HEADS = N_HEADS_TOTAL - NA_HEADS
GQA_KV_HEADS = max(1, GQA_HEADS // 4)
NA_WIDTH = NA_HEADS * HEAD_DIM
GQA_WIDTH = GQA_HEADS * HEAD_DIM
GQA_KV_WIDTH = GQA_KV_HEADS * HEAD_DIM
MIX_WIDTH = NA_WIDTH + GQA_WIDTH
IN_PROJ_WIDTH = 3 * NA_WIDTH + GQA_WIDTH + 2 * GQA_KV_WIDTH
GRID_W = 64
NA_KH_MAX = 8
NA_KW = 16
Q_BLOCK = 128
ROPE_THETA = 10000.0
D_FF = ((8 * D_MODEL // 3) + 255) // 256 * 256
CONV_W = 3
EPS = 1e-6

kernel_name = "hybrid_natten_gqa_convffn_encoder"

def rms_norm(x, g):
    xf = x.astype(jnp.float32)
    y = xf * lax.rsqrt(jnp.mean(xf * xf, axis=-1, keepdims=True) + EPS)
    return (y * g.astype(jnp.float32)).astype(x.dtype)

def neighbourhood_attention(q, k, v, rpb):
    B, S, H, Dh = q.shape
    rows = S // GRID_W
    kh = min(NA_KH_MAX, rows)
    qg = q.reshape(B, rows, GRID_W, H, Dh)
    kg = k.reshape(B, rows, GRID_W, H, Dh)
    vg = v.reshape(B, rows, GRID_W, H, Dh)
    r = jnp.arange(rows)
    row_start = jnp.clip(r - kh // 2, 0, rows - kh)
    row_idx = row_start[:, None] + jnp.arange(kh)[None, :]
    c = jnp.arange(GRID_W)
    col_start = jnp.clip(c - NA_KW // 2, 0, GRID_W - NA_KW)
    col_in = (c[None, :] >= col_start[:, None]) & (c[None, :] < col_start[:, None] + NA_KW)
    k_rows = kg[:, row_idx]
    v_rows = vg[:, row_idx]
    scores = jnp.einsum('brqhd,brikhd->bhrqik', qg, k_rows).astype(jnp.float32) * (HEAD_DIM ** -0.5)
    dr = row_idx - r[:, None] + (NA_KH_MAX - 1)
    dc = jnp.clip(c[None, :] - c[:, None], -(NA_KW - 1), NA_KW - 1) + (NA_KW - 1)
    bias = rpb.astype(jnp.float32)[:, dr[:, None, :, None], dc[None, :, None, :]]
    bias = jnp.where(col_in[:, None, :], bias, -jnp.inf)
    scores = scores + bias[None]
    p = jax.nn.softmax(scores.reshape(B, H, rows, GRID_W, kh * GRID_W), axis=-1)
    p = p.reshape(B, H, rows, GRID_W, kh, GRID_W).astype(v.dtype)
    out = jnp.einsum('bhrqik,brikhd->brqhd', p, v_rows)
    return out.reshape(B, S, H, Dh)

def axial_rope_tables(S):
    t = jnp.arange(S)
    row = (t // GRID_W).astype(jnp.float32)
    col = (t % GRID_W).astype(jnp.float32)
    axis_dim = HEAD_DIM // 2
    inv_freq = 1.0 / (ROPE_THETA ** (jnp.arange(0, axis_dim, 2, dtype=jnp.float32) / axis_dim))
    ang = jnp.concatenate([row[:, None] * inv_freq[None, :], col[:, None] * inv_freq[None, :]], axis=-1)
    return jnp.cos(ang), jnp.sin(ang)

def apply_rope(x, cos, sin):
    xf = x.astype(jnp.float32).reshape(*x.shape[:-1], HEAD_DIM // 2, 2)
    x0, x1 = xf[..., 0], xf[..., 1]
    cb = cos[None, :, None, :]
    sb = sin[None, :, None, :]
    out = jnp.stack([x0 * cb - x1 * sb, x0 * sb + x1 * cb], axis=-1)
    return out.reshape(x.shape).astype(x.dtype)

def gqa_attention(q, k, v):
    B, S, Hq, Dh = q.shape
    Hkv = k.shape[2]
    g = Hq // Hkv
    nb = S // Q_BLOCK
    qb = q.reshape(B, nb, Q_BLOCK, Hkv, g, Dh).transpose(1, 0, 2, 3, 4, 5)

    def block(qi):
        s = jnp.einsum('bqkgd,bskd->bkgqs', qi, k).astype(jnp.float32) * (HEAD_DIM ** -0.5)
        p = jax.nn.softmax(s, axis=-1).astype(v.dtype)
        return jnp.einsum('bkgqs,bskd->bqkgd', p, v)

    o = lax.map(block, qb)
    return o.transpose(1, 0, 2, 3, 4, 5).reshape(B, S, Hq, Dh)

def depthwise_conv_centred(u, w, b):
    C = u.shape[-1]
    y = lax.conv_general_dilated(
        u, w[:, None, :].astype(u.dtype), window_strides=(1,),
        padding=[(CONV_W // 2, CONV_W // 2)],
        dimension_numbers=('NWC', 'WIO', 'NWC'), feature_group_count=C)
    return y + b.astype(u.dtype)

def hybrid_layer(x, ln1_g, w_in, na_rpb, q_norm_g, k_norm_g, na_out_g, gqa_out_g,
                 w_out, ln2_g, w_up, conv_w, conv_b, w_down, cos, sin):
    B, S, _ = x.shape
    h = rms_norm(x, ln1_g)
    proj = h @ w_in
    o1 = NA_WIDTH
    o2 = o1 + NA_WIDTH
    o3 = o2 + NA_WIDTH
    o4 = o3 + GQA_WIDTH
    o5 = o4 + GQA_KV_WIDTH
    na_q = proj[..., :o1].reshape(B, S, NA_HEADS, HEAD_DIM)
    na_k = proj[..., o1:o2].reshape(B, S, NA_HEADS, HEAD_DIM)
    na_v = proj[..., o2:o3].reshape(B, S, NA_HEADS, HEAD_DIM)
    g_q = proj[..., o3:o4].reshape(B, S, GQA_HEADS, HEAD_DIM)
    g_k = proj[..., o4:o5].reshape(B, S, GQA_KV_HEADS, HEAD_DIM)
    g_v = proj[..., o5:].reshape(B, S, GQA_KV_HEADS, HEAD_DIM)

    na_o = neighbourhood_attention(na_q, na_k, na_v, na_rpb).reshape(B, S, NA_WIDTH)

    g_q = apply_rope(rms_norm(g_q, q_norm_g), cos, sin)
    g_k = apply_rope(rms_norm(g_k, k_norm_g), cos, sin)
    gqa_o = gqa_attention(g_q, g_k, g_v).reshape(B, S, GQA_WIDTH)

    mixed = jnp.concatenate([rms_norm(na_o, na_out_g), rms_norm(gqa_o, gqa_out_g)], axis=-1)
    x = x + mixed @ w_out

    h2 = rms_norm(x, ln2_g)
    u = depthwise_conv_centred(h2 @ w_up, conv_w, conv_b)
    gate = u[..., :D_FF]
    val = u[..., D_FF:]
    x = x + (jax.nn.silu(gate) * val) @ w_down
    return x

def setup_inputs(seed: int = 0) -> dict:
    key = jax.random.key(seed)
    ks = jax.random.split(key, 16)
    f32 = jnp.float32

    def nrm(k, shape, scale):
        return jax.random.normal(k, shape, f32) * scale

    def gain(k, shape):
        return 1.0 + 0.02 * jax.random.normal(k, shape, f32)

    return {
        "x": jax.random.normal(ks[0], (BATCH, SEQ, D_MODEL), f32),
        "ln1_g": gain(ks[1], (DEPTH, D_MODEL)),
        "w_in": nrm(ks[2], (DEPTH, D_MODEL, IN_PROJ_WIDTH), D_MODEL ** -0.5),
        "na_rpb": nrm(ks[3], (DEPTH, NA_HEADS, 2 * NA_KH_MAX - 1, 2 * NA_KW - 1), 0.1),
        "q_norm_g": gain(ks[4], (DEPTH, HEAD_DIM)),
        "k_norm_g": gain(ks[5], (DEPTH, HEAD_DIM)),
        "na_out_g": gain(ks[6], (DEPTH, NA_WIDTH)),
        "gqa_out_g": gain(ks[7], (DEPTH, GQA_WIDTH)),
        "w_out": nrm(ks[8], (DEPTH, MIX_WIDTH, D_MODEL), MIX_WIDTH ** -0.5),
        "ln2_g": gain(ks[9], (DEPTH, D_MODEL)),
        "w_up": nrm(ks[10], (DEPTH, D_MODEL, 2 * D_FF), D_MODEL ** -0.5),
        "conv_w": nrm(ks[11], (DEPTH, CONV_W, 2 * D_FF), CONV_W ** -0.5),
        "conv_b": nrm(ks[12], (DEPTH, 2 * D_FF), 0.02),
        "w_down": nrm(ks[13], (DEPTH, D_FF, D_MODEL), D_FF ** -0.5),
        "final_g": gain(ks[14], (D_MODEL,)),
    }

def reference(x, ln1_g, w_in, na_rpb, q_norm_g, k_norm_g, na_out_g, gqa_out_g,
              w_out, ln2_g, w_up, conv_w, conv_b, w_down, final_g):
    S = x.shape[1]
    cos, sin = axial_rope_tables(S)
    for l in range(DEPTH):
        x = hybrid_layer(x, ln1_g[l], w_in[l], na_rpb[l], q_norm_g[l], k_norm_g[l],
                         na_out_g[l], gqa_out_g[l], w_out[l], ln2_g[l], w_up[l],
                         conv_w[l], conv_b[l], w_down[l], cos, sin)
    return rms_norm(x, final_g)


_drawn_inputs = setup_inputs


def setup_inputs(seed=0):
    import zlib

    import numpy as np

    out = dict(_drawn_inputs(seed))
    spreads = {}
    factors = {'q_norm_g': 5.338,
     'k_norm_g': 4.671,
     'na_out_g': 5.085,
     'gqa_out_g': 5.213,
     'ln2_g': 4.785,
     'conv_b': 5.165,
     'final_g': 2.792}
    for name, (base, spread) in spreads.items():
        noise = np.random.default_rng([zlib.crc32(name.encode()), seed]).standard_normal(out[name].shape)
        drawn = base * np.exp(spread * noise) if base else spread * noise
        out[name] = __import__('jax').numpy.asarray(drawn.astype(out[name].dtype))
    for name, factor in factors.items():
        out[name] = (out[name] * factor).astype(out[name].dtype)
    return out
```

```python
from contextlib import ExitStack

import concourse.bass as bass
from concourse import mybir
from concourse.alu_op_type import AluOpType as ALU

ACT = mybir.ActivationFunctionType
AX = mybir.AxisListType
F32 = mybir.dt.float32
F32R = mybir.dt.float32r

P = 128
D = 2048
S = 256
T = S // P
KT = D // P
DH = 128
NAH = 8
GH = 8
GKV = 2
GW = 64
ROWS = S // GW
RPB_R, RPB_C = 15, 31
FF = 5632
FT = FF // P
EPS = 1e-6
SCALE = float(DH) ** -0.5
MASKED = -1.0e30

RAW = 4
HIS = 2
G_GQA = 0
G_NAV = G_GQA + 12
G_NAQK = G_NAV + 8
G_OUT = G_NAQK + 16
G_UP = G_OUT + 16
UPC = FF // 256
G_DOWN = G_UP + 4 * UPC
DNB = FT // 4
G_END = G_DOWN + 4 * DNB

C_OUT = 13
C_UP = C_OUT + 8

A_SCORES = 23
A_TRANSPOSE = A_SCORES + 2
A_PV = A_SCORES + 3
A_SUMSQ = A_SCORES + 5
HEADS = GH + NAH

LN1, LN2, NAG, GQAG = 0, KT, 2 * KT, 2 * KT + NAH
CONV = 2 * KT + NAH + GH
PARAMS = CONV + 4 * 2 * FT


def hybrid_block(nc, x, ln1_g, w_in, na_rpb, q_norm_g, k_norm_g, na_out_g, gqa_out_g, w_out,
                 ln2_g, w_up, conv_w, conv_b, w_down, final_g, cos_t, sin_t, out):
    with ExitStack() as ctx:
        sem = lambda name: ctx.enter_context(nc.semaphore(name))

        BASE = 16512
        A_RES = BASE
        A_X = A_RES + T * D * 4
        A_E = A_X + KT * 2 * S * 4
        A_O = A_E + 57344
        A_RAW = A_O + KT * 2 * S * 4
        A_HI = A_RAW + RAW * 8192
        A_M = A_HI + HIS * 8192

        def at(name, shape, dt, offset):
            return nc.alloc_sbuf_tensor_at(name, shape, dt, offset=offset)

        res = at("res", [P, T, D], F32, A_RES)
        xT = at("xT", [P, KT, 2 * S], F32R, A_X)
        naqkT = at("naqkT", [P, 2 * NAH, S], F32, A_E)
        nav = at("nav", [P, T, NAH * DH], F32, A_E + 16384)
        gproj = at("gproj", [P, T, 1536], F32, A_E + 24576)
        gT = at("gT", [P, GH + GKV, S], F32, A_E + 36864)
        prob = at("prob", [P, 2, T, S], F32, A_E + 47104)
        probT = at("probT", [P, 2, T, S], F32, A_E + 51200)
        osq = at("osq", [P, 2, S], F32, A_E + 55296)
        oT = at("oT", [P, KT, 2 * S], F32R, A_O)
        h2T = at("h2T", [P, KT, 2 * S], F32R, A_O)
        xn = at("xn", [P, T, D], F32, A_O)
        h2n = at("h2n", [P, T, D], F32, A_E)
        stage = at("stage", [P, 5, P], F32, A_O + 16384)
        rot_n = at("rot_n", [P, 10, DH], F32, A_O + 16384)
        rot_m = at("rot_m", [P, 10, DH], F32, A_O + 16384 + 5120)
        cosr = at("cosr", [P, T, DH], F32, A_O + 26624)
        sinr = at("sinr", [P, T, DH], F32, A_O + 27648)
        grow = at("grow", [P, 2, DH], F32, A_O + 28672)
        actT = at("actT", [P, FT, 2 * S], F32R, A_X)
        fgain = at("fgain", [P, D], F32, A_O)
        junk = at("junk", [P, T, D], F32, A_O + 8192)
        raw = at("raw", [P, RAW, 2048], F32, A_RAW)
        wlo = at("wlo", [P, RAW, 2048], F32R, A_RAW)
        whi = at("whi", [P, HIS, 2048], F32R, A_HI)
        par = at("par", [P, PARAMS], F32, A_M)
        stat = at("stat", [P, 256], F32, A_M + 1600)
        ident = at("ident", [P, P], F32, A_M + 2624)
        ones = at("ones", [P, 1], F32, A_M + 3136)
        eps = at("eps", [P, 1], F32, A_M + 3168)
        A_W = A_M + 3200
        bias = at("bias", [P, NAH, 6, GW], F32, A_W)
        u = at("u", [P, 2, 2, S + 2], F32, A_W)
        y = at("y", [P, 2, 2, S], F32, A_W + 4160)
        prod = at("prod", [P, 2, S], F32, A_W + 8256)
        cosg = at("cosg", [P, T, 2, DH], F32, A_W + 12288)
        sing = at("sing", [P, T, 2, DH], F32, A_W + 14336)
        biased = at("biased", [P, T, S], F32, A_W + 16384)
        cross = at("cross", [P, 2, S], F32, A_W + 18432)

        ps = ctx.enter_context(nc.psum_tensor("ps", [P, 8, 512], F32))
        scores_ps = ps[:, 4, :].rearrange("p (t k) -> p t k", t=T)
        probT_ps = ps[:, 5, :].rearrange("p (k q) -> p k q", k=T)

        ssq1, std1, rs1 = stat[:, 0:2], stat[:, 2:4], stat[:, 4:6]
        ssq2p = stat[:, 8:16].rearrange("p (t c) -> p t c", t=T)
        ssq2, std2, rs2 = stat[:, 16:18], stat[:, 18:20], stat[:, 20:22]
        ssq3, std3, rs3 = stat[:, 24:26], stat[:, 26:28], stat[:, 28:30]
        ssqg = stat[:, 32:52].rearrange("p (t h) -> p t h", t=T)
        stdg = stat[:, 52:72].rearrange("p (t h) -> p t h", t=T)
        rsg = stat[:, 72:92].rearrange("p (t h) -> p t h", t=T)
        ssqo = stat[:, 96:100].rearrange("p (g t) -> p g t", g=2)
        stdo = stat[:, 100:104].rearrange("p (g t) -> p g t", g=2)
        rso = stat[:, 104:108].rearrange("p (g t) -> p g t", g=2)
        smax = stat[:, 112:144].rearrange("p (a t) -> p a t", t=T)
        nmax = stat[:, 144:176].rearrange("p (a t) -> p a t", t=T)
        esum = stat[:, 176:208].rearrange("p (a t) -> p a t", t=T)
        rsum = stat[:, 208:240].rearrange("p (a t) -> p a t", t=T)
        headsq_ps = ps[:, 7, 0:2 * HEADS].rearrange("p (a t) -> p a t", t=T)

        x_loaded = [sem(f"x_loaded{t}") for t in range(T)]
        params_loaded = sem("params_loaded")
        rope_loaded = sem("rope_loaded")
        bias_loaded = sem("bias_loaded")
        fgain_loaded = sem("fgain_loaded")
        stored = sem("stored")
        w_loaded = [sem(f"w_loaded{i}") for i in range(RAW)]
        hi_ready = sem("hi_ready")
        lo_ready = sem("lo_ready")
        granule_used = sem("granule_used")
        banks_free = sem("banks_free")
        ident_zero, ident_ready = sem("ident_zero"), sem("ident_ready")
        ones_ready, eps_ready = sem("ones_ready"), sem("eps_ready")
        bias_masked = sem("bias_masked")
        par_in_psum, par_ready = sem("par_in_psum"), sem("par_ready")
        squared, std_ready, stat_ready = sem("squared"), sem("std_ready"), sem("stat_ready")
        normed = sem("normed")
        tile_turned = sem("tile_turned")
        tile_hi, tile_lo = sem("tile_hi"), sem("tile_lo")
        cross_copied = sem("cross_copied")
        tables_ready = sem("tables_ready")
        rope_step = sem("rope_step")
        stdg_ready = sem("stdg_ready")
        g_turned, g_copied = sem("g_turned"), sem("g_copied")
        scored = sem("scored")
        biased_ready = sem("biased_ready")
        max_ready, nmax_ready = sem("max_ready"), sem("nmax_ready")
        exp_done = sem("exp_done")
        rsum_ready, prob_ready = sem("rsum_ready"), sem("prob_ready")
        prob_turned, probT_ready = sem("prob_turned"), sem("probT_ready")
        pv_done = sem("pv_done")
        osq_ready, o_hi, o_lo = sem("osq_ready"), sem("o_hi"), sem("o_lo")
        head_summed = sem("head_summed")
        osum_ready, ostd_ready, ors_ready = sem("osum_ready"), sem("ostd_ready"), sem("ors_ready")
        pads_zero = sem("pads_zero")
        centre_ready = sem("centre_ready")
        tap_done, conv_ready = sem("tap_done"), sem("conv_ready")
        silu_ready, prod_ready = sem("silu_ready"), sem("prod_ready")
        act_hi, act_lo = sem("act_hi"), sem("act_lo")
        down_done, x2_ready, y_ready = sem("down_done"), sem("x2_ready"), sem("y_ready")

        w_in_v = w_in[0].rearrange("(k p) n -> p k n", p=P)
        w_out_v = w_out[0].rearrange("(k p) n -> p k n", p=P)
        w_up_v = w_up[0].rearrange("(k p) n -> p k n", p=P)
        w_down_v = w_down[0].rearrange("(b k p) n -> b p k n", p=P, k=4)
        NA_W = NAH * DH

        def source(g):
            if g < G_NAQK:
                c, kq = divmod(g, 4)
                col = 3 * NA_W + 512 * c if c < 3 else 2 * NA_W + 512 * (c - 3)
                return w_in_v[:, 4 * kq:4 * kq + 4, col:col + 512]
            if g < G_OUT:
                c, kh = divmod(g - G_NAQK, 2)
                col = (c % 2) * NA_W + 256 * (c // 2)
                return w_in_v[:, 8 * kh:8 * kh + 8, col:col + 256]
            c, kh = divmod(g - G_OUT, 2)
            k = (NAH if c < 4 else 0) + 4 * kh
            return w_out_v[:, k:k + 4, 512 * (c % 4):512 * (c % 4) + 512]

        block = ctx.enter_context(nc.Block())

        @block.sync
        def _(sp):
            xv = x[0].rearrange("(t p) d -> p t d", p=P)
            for t in range(T):
                sp.dma_start(res[:, t, :], xv[:, t, :]).then_inc(x_loaded[t], 16)

            def load(slot, src):
                k = src.shape[1]
                dst = raw[:, slot, :].rearrange("p (k n) -> p k n", k=k)
                sp.dma_start(dst, src).then_inc(w_loaded[slot], 16)

            for g in range(G_UP):
                if g >= RAW:
                    sp.wait_ge(granule_used, g - RAW + 1)
                load(g % RAW, source(g))
            with sp.Fori(0, UPC) as c:
                for j in range(4):
                    sp.wait_ge(granule_used, c * 4 + (G_UP + j - RAW + 1))
                    col = c * 256 + (j // 2) * FF
                    load((G_UP + j) % RAW, w_up_v[:, 8 * (j % 2):8 * (j % 2) + 8, bass.ds(col, 256)])
            with sp.Fori(0, DNB) as b:
                for j in range(4):
                    sp.wait_ge(granule_used, b * 4 + (G_DOWN + j - RAW + 1))
                    src = w_down_v[bass.ds(b, 1), :, :, 512 * j:512 * j + 512].rearrange(
                        "o p k n -> (o p) k n")
                    load((G_DOWN + j) % RAW, src)
            sp.dma_start(fgain[:, :], final_g.rearrange("(o d) -> o d", o=1).broadcast_to([P, D]))\
                .then_inc(fgain_loaded, 16)
            ov = out[0].rearrange("(t p) d -> p t d", p=P)
            for t in range(T):
                sp.wait_ge(y_ready, t + 1)
                sp.dma_start(ov[:, t, :], res[:, t, :]).then_inc(stored, 16)
            sp.wait_ge(stored, 16 * T)

        @block.gpsimd
        def _(pool):
            pool.memset(ones[:, :], 1.0).then_inc(ones_ready, 1)
            pool.memset(ident[:, :], 0.0).then_inc(ident_zero, 1)
            pool.wait_ge(ident_zero, 1)
            pool.affine_select(out=ident[:, :], in_=ident[:, :], compare_op=ALU.not_equal, fill=1.0,
                               base=0, pattern=[[-1, P]], channel_multiplier=1).then_inc(ident_ready, 1)
            pool.wait_ge(bias_loaded, 16 * 2 * NAH)
            n = 0
            for half in range(2):
                b = bias[GW * half:GW * half + GW].rearrange("p h j m -> p (h j) m")
                left, right = b[:, :, 16:64], b[:, :, 0:48]
                pool.affine_select(out=left, in_=left, compare_op=ALU.is_ge, fill=MASKED, base=55,
                                   pattern=[[0, 6 * NAH], [-1, 48]], channel_multiplier=-1)\
                    .then_inc(bias_masked, 1)
                n += 1
                pool.wait_ge(bias_masked, n)
                pool.affine_select(out=right, in_=right, compare_op=ALU.is_ge, fill=MASKED, base=-56,
                                   pattern=[[0, 6 * NAH], [1, 48]], channel_multiplier=1)\
                    .then_inc(bias_masked, 1)
                n += 1

        @block.scalar
        def _(act):
            row = 0
            for vec, rows in ((ln1_g, KT), (ln2_g, KT), (na_out_g, NAH), (gqa_out_g, GH)):
                act.dma_start(stage[row:row + rows, 0, :], vec[0].rearrange("(f p) -> f p", p=P))\
                    .then_inc(params_loaded, 16)
                row += rows
            for j in range(4):
                vec = conv_w[0, j, :] if j < 3 else conv_b[0]
                act.dma_start(stage[0:2 * FT, 1 + j, :], vec.rearrange("(f p) -> f p", p=P))\
                    .then_inc(params_loaded, 16)
            for i, vec in enumerate((q_norm_g, k_norm_g)):
                act.dma_start(grow[:, i, :], vec.broadcast_to([P, DH])).then_inc(rope_loaded, 16)
            act.dma_start(cosr[:, :, :], cos_t.rearrange("(t p) d -> p t d", p=P)).then_inc(rope_loaded, 16)
            act.dma_start(sinr[:, :, :], sin_t.rearrange("(t p) d -> p t d", p=P)).then_inc(rope_loaded, 16)
            for t in range(T):
                act.wait_ge(x_loaded[t], 16)
                act.activation(xn[:, t, :], res[:, t, :], ACT.Square, accum_out=ssq1[:, t:t + 1])\
                    .then_inc(squared, 1)
            act.wait_ge(squared, T)
            act.wait_ge(eps_ready, 1)
            act.activation(std1, ssq1, ACT.Sqrt, bias=eps[:, :], scale=1.0 / D).then_inc(std_ready, 1)
            for half in range(2):
                for h in range(NAH):
                    off = h * RPB_R * RPB_C + (5 - half) * RPB_C + 15 - (GW - 1)
                    src = bass.AP(na_rpb.tensor, off, [[1, GW], [RPB_C, 6], [1, GW]])
                    act.dma_start(bias[GW * half:GW * half + GW, h], src).then_inc(bias_loaded, 16)

            def split_hi(slot_raw, slot_hi, loaded, used):
                act.wait_ge(w_loaded[slot_raw], loaded)
                if used is not None:
                    act.wait_ge(granule_used, used)
                act.activation(whi[:, slot_hi, :], raw[:, slot_raw, :], ACT.Copy).then_inc(hi_ready, 1)

            def split_at(g):
                split_hi(g % RAW, g % HIS, 16 * (g // RAW + 1), g - HIS + 1 if g >= HIS else None)

            def turned_hi(dst, gain0, n0):
                for k in range(KT):
                    act.wait_ge(tile_turned, n0 + k + 2 - k % 2)
                    b, h = 4 + (k // 2) % 4, k % 2
                    act.activation(dst[:, k, 0:S], ps[:, b, S * h:S * h + S], ACT.Copy,
                                   scale=par[:, gain0 + k:gain0 + k + 1]).then_inc(tile_hi, 1)

            split_at(0)
            act.wait_ge(par_ready, 1)
            turned_hi(xT, LN1, 0)
            for g in range(1, G_UP + 2):
                split_at(g)
                c = (g - G_NAQK - 3) // 2
                if (g - G_NAQK - 3) % 2 == 0 and 0 <= c < 8:
                    act.wait_ge(granule_used, g - 1)
                    if c >= 1:
                        act.wait_ge(banks_free, 5 + c)
                    b = 2 * ((5 + c) % 2)
                    act.activation(cross[:, :, :], ps[:, b:b + 2, S:2 * S], ACT.Copy).then_inc(cross_copied, 1)
                if g == 15:
                    act.wait_ge(rope_step, 4)
                    act.activation(stdg, ssqg, ACT.Sqrt, bias=eps[:, :], scale=1.0 / DH).then_inc(stdg_ready, 1)
                if 22 <= g < 27:
                    i = g - 22
                    act.wait_ge(g_turned, i + 1)
                    h0 = (2 * (i - 1)) % 10
                    act.activation(gT[:, h0:h0 + 2, :], ps[:, 7, :].rearrange("p (h s) -> p h s", h=2),
                                   ACT.Copy).then_inc(g_copied, 1)
                a = g - A_SCORES - 2
                if 0 <= a < HEADS:
                    act.wait_ge(nmax_ready, a + 1)
                    if a >= 2:
                        act.wait_ge(prob_turned, a - 1)
                    for t in range(T):
                        src, sc = (scores_ps, SCALE) if a < GH else (biased, 1.0)
                        act.activation(prob[:, a % 2, t, :], src[:, t, :], ACT.Exp, bias=nmax[:, a, t:t + 1],
                                       scale=sc, accum_out=esum[:, a, t:t + 1]).then_inc(exp_done, 1)
                a = g - A_TRANSPOSE - 2
                if 0 <= a < HEADS:
                    act.wait_ge(prob_turned, a + 1)
                    if a >= 2:
                        act.wait_ge(pv_done, a - 1)
                    act.activation(probT[:, a % 2], probT_ps, ACT.Copy).then_inc(probT_ready, 1)
                a = g - A_PV - 2
                if 0 <= a < HEADS:
                    act.wait_ge(pv_done, a + 1)
                    if a >= 2:
                        act.wait_ge(head_summed, a - 1)
                    o = ps[:, 6, 0:S]
                    act.activation(osq[:, a % 2, :], o, ACT.Square).then_inc(osq_ready, 1)
                    tile = (a + NAH) % KT
                    act.activation(oT[:, tile, 0:S], o, ACT.Copy, scale=par[:, NAG + tile:NAG + tile + 1])\
                        .then_inc(o_hi, 1)
                for i, last in ((0, GH), (1, HEADS)):
                    if g == A_SUMSQ + last - 1 + 2:
                        act.wait_ge(osum_ready, i + 1)
                        act.activation(stdo[:, i, :], ssqo[:, i, :], ACT.Sqrt, bias=eps[:, :],
                                       scale=1.0 / (NAH * DH)).then_inc(ostd_ready, 1)
                c = (g - G_OUT - 3) // 2
                if (g - G_OUT - 3) % 2 == 0 and 4 <= c < 8:
                    act.wait_ge(banks_free, C_OUT + c + 1)
                    if c == 4:
                        act.wait_ge(pv_done, HEADS)
                    for t in range(T):
                        cs = slice(512 * (c - 4), 512 * (c - 4) + 512)
                        act.activation(h2n[:, t, cs], res[:, t, cs], ACT.Square,
                                       accum_out=ssq2p[:, t, c - 4:c - 3]).then_inc(squared, 1)
            act.wait_ge(stat_ready, 2)
            act.activation(std2, ssq2, ACT.Sqrt, bias=eps[:, :], scale=1.0 / D).then_inc(std_ready, 1)
            turned_hi(h2T, LN2, KT)
            split_at(G_UP + 2)

            with act.Fori(0, UPC) as c:
                for j in range(4):
                    g = G_UP + 3 + j
                    split_hi(g % RAW, g % HIS, c * 16 + 16 * (g // RAW + 1), c * 4 + (g - HIS + 1))
                    half = j // 2
                    if j % 2 == 0:
                        b = 2 * ((C_UP + half) % 2)
                        act.wait_ge(granule_used, c * 4 + (G_UP + 2 * half + 2))
                        act.wait_ge(banks_free, c * 2 + (C_UP + half))
                        act.activation(cross[:, :, :], ps[:, b:b + 2, S:2 * S], ACT.Copy)\
                            .then_inc(cross_copied, 1)
                        continue
                    act.wait_ge(banks_free, c * 2 + (C_UP + half + 1))
                    for f in range(2):
                        col = c * 2 + (CONV + 2 * FT + half * FT + f)
                        act.activation(y[:, half, f, :], u[:, half, f, 1:S + 1], ACT.Identity,
                                       scale=par[:, bass.ds(col, 1)],
                                       bias=par[:, bass.ds(col + 2 * 2 * FT, 1)]).then_inc(centre_ready, 1)
                    if half == 0:
                        continue
                    act.wait_ge(conv_ready, c * 4 + 2)
                    act.activation(y[:, 0], y[:, 0], ACT.Silu).then_inc(silu_ready, 1)
                    act.wait_ge(prod_ready, c + 1)
                    act.activation(actT[:, bass.ds(c * 2, 2), 0:S], prod[:, :, :], ACT.Copy)\
                        .then_inc(act_hi, 1)
            split_at(G_DOWN + 3)
            with act.Fori(0, DNB - 1) as b:
                for j in range(4):
                    g = G_DOWN + 4 + j
                    split_hi(g % RAW, g % HIS, b * 16 + 16 * (g // RAW + 1), b * 4 + (g - HIS + 1))
            for t in range(T):
                act.wait_ge(x2_ready, 4 * (t + 1))
                act.activation(junk[:, t, :], res[:, t, :], ACT.Square, accum_out=ssq3[:, t:t + 1])\
                    .then_inc(squared, 1)
            act.wait_ge(squared, T + 8 + T)
            act.activation(std3, ssq3, ACT.Sqrt, bias=eps[:, :], scale=1.0 / D).then_inc(std_ready, 1)

        @block.vector
        def _(dve):
            dve.memset(eps[:, :], EPS).then_inc(eps_ready, 1)
            def split_lo(slot_raw, slot_hi, ready):
                dve.wait_ge(hi_ready, ready)
                dve.tensor_tensor(wlo[:, slot_raw, :], raw[:, slot_raw, :], whi[:, slot_hi, :].bitcast(F32),
                                  ALU.subtract).then_inc(lo_ready, 1)

            def split_at(g):
                split_lo(g % RAW, g % HIS, g + 1)

            def turned_lo(dst, gain0, n0):
                for k in range(KT):
                    dve.wait_ge(tile_hi, n0 + k + 2 - k % 2)
                    b, h = 4 + (k // 2) % 4, k % 2
                    dve.scalar_tensor_tensor(out=dst[:, k, S:2 * S], in0=ps[:, b, S * h:S * h + S],
                                             scalar=par[:, gain0 + k:gain0 + k + 1],
                                             in1=dst[:, k, 0:S].bitcast(F32), op0=ALU.mult,
                                             op1=ALU.subtract).then_inc(tile_lo, 1)

            dve.wait_ge(par_in_psum, 1)
            dve.tensor_copy(par[:, :], ps[:, 0, 0:PARAMS]).then_inc(par_ready, 1)
            dve.wait_ge(std_ready, 1)
            dve.reciprocal(rs1, std1).then_inc(stat_ready, 1)
            dve.wait_ge(stat_ready, 1)
            for t in range(T):
                dve.tensor_scalar(xn[:, t, :], res[:, t, :], rs1[:, t:t + 1], None, ALU.mult)\
                    .then_inc(normed, 1)
            split_at(0)
            turned_lo(xT, LN1, 0)

            dve.wait_ge(rope_loaded, 64)
            for t in range(T):
                for i in range(2):
                    dve.tensor_tensor(cosg[:, t, i, :], cosr[:, t, :], grow[:, i, :], ALU.mult)\
                        .then_inc(tables_ready, 1)
                    for e in range(2):
                        dve.tensor_tensor(sing[:, t, i, e::2], sinr[:, t, e::2], grow[:, i, 1 - e::2],
                                          ALU.mult).then_inc(tables_ready, 1)

            def over_heads(table, n):
                return table.unsqueeze(1).broadcast_to([P, n, table.shape[1]])

            groups = ((0, 0, GH), (1, GH, GKV))

            def rope(step, t):
                heads = gproj[:, t, 0:10 * DH].rearrange("p (h d) -> p h d", d=DH)
                if step == 0:
                    if t == 1:
                        dve.wait_ge(rope_step, 2)
                    dve.tensor_tensor(rot_n[:, :, :], heads, heads, ALU.mult).then_inc(rope_step, 1)
                    dve.wait_ge(rope_step, 2 * t + 1)
                    dve.tensor_reduce(ssqg[:, t, :], rot_n[:, :, :], AX.X, ALU.add).then_inc(rope_step, 1)
                if step == 1:
                    base = 4 + 7 * t
                    if t == 0:
                        dve.wait_ge(stdg_ready, 1)
                        dve.reciprocal(rsg, stdg).then_inc(rope_step, 1)
                        dve.wait_ge(rope_step, 5)
                        dve.wait_ge(tables_ready, 12)
                    base = 5 + 8 * t
                    dve.wait_ge(rope_step, base)
                    dve.tensor_tensor(rot_n[:, :, :], heads, rsg[:, t, :].unsqueeze(2).broadcast_to([P, 10, DH]),
                                      ALU.mult).then_inc(rope_step, 1)
                    dve.wait_ge(rope_step, base + 1)
                    for i, h0, n in groups:
                        for e in range(2):
                            dve.tensor_tensor(rot_m[:, h0:h0 + n, e::2], rot_n[:, h0:h0 + n, 1 - e::2],
                                              over_heads(sing[:, t, i, e::2], n), ALU.mult)\
                                .then_inc(rope_step, 1)
                if step == 2:
                    base = 5 + 8 * t + 5
                    dve.wait_ge(rope_step, base)
                    for i, h0, n in groups:
                        dve.tensor_tensor(rot_n[:, h0:h0 + n, :], rot_n[:, h0:h0 + n, :],
                                          over_heads(cosg[:, t, i, :], n), ALU.mult).then_inc(rope_step, 1)
                    dve.wait_ge(rope_step, base + 2)
                    dve.tensor_tensor(heads, rot_n[:, :, :], rot_m[:, :, :], ALU.add).then_inc(rope_step, 1)

            for g in range(1, G_UP + 2):
                split_at(g)
                c = (g - 5) // 4
                if (g - 5) % 4 == 0 and 0 <= c < 5:
                    dve.wait_ge(granule_used, g - 1)
                    b = 2 * (c % 2)
                    dst = gproj[:, :, 512 * c:512 * c + 512] if c < 3 else \
                        nav[:, :, 512 * (c - 3):512 * (c - 3) + 512]
                    dve.tensor_copy(dst, ps[:, b:b + 2, :]).then_inc(banks_free, 1)
                c = (g - G_NAQK - 3) // 2
                if (g - G_NAQK - 3) % 2 == 0 and 0 <= c < 8:
                    dve.wait_ge(cross_copied, c + 1)
                    b = 2 * ((5 + c) % 2)
                    dve.tensor_tensor(naqkT[:, 2 * c:2 * c + 2, :], ps[:, b:b + 2, 0:S], cross[:, :, :],
                                      ALU.add).then_inc(banks_free, 1)
                for i, (step, t) in enumerate(((0, 0), (0, 1), (1, 0), (2, 0), (1, 1), (2, 1))):
                    if g == 14 + i:
                        if i == 0:
                            dve.wait_ge(banks_free, 3)
                        rope(step, t)
                a = g - A_SCORES - 2
                if 0 <= a < HEADS:
                    dve.wait_ge(scored, a + 1)
                    if a < GH:
                        dve.tensor_reduce(smax[:, a, :], scores_ps, AX.X, ALU.max).then_inc(max_ready, 1)
                        dve.wait_ge(max_ready, a + 1)
                        dve.tensor_scalar(nmax[:, a, :], smax[:, a, :], -SCALE, None, ALU.mult)\
                            .then_inc(nmax_ready, 1)
                    else:
                        n = a - GH
                        if n == 0:
                            dve.wait_ge(bias_masked, 4)
                        for t in range(T):
                            j0 = 2 - 2 * t
                            rev = bass.AP(bias, (n * 6 + j0) * GW + GW - 1,
                                          [[NAH * 6 * GW, P], [GW, ROWS], [-1, GW]])
                            dve.scalar_tensor_tensor(
                                out=biased[:, t, :].rearrange("p (r m) -> p r m", r=ROWS),
                                in0=scores_ps[:, t, :].rearrange("p (r m) -> p r m", r=ROWS),
                                scalar=SCALE, in1=rev, op0=ALU.mult, op1=ALU.add).then_inc(biased_ready, 1)
                        dve.wait_ge(biased_ready, 2 * n + 2)
                        dve.tensor_reduce(nmax[:, a, :], biased[:, :, :], AX.X, ALU.max, negate=True)\
                            .then_inc(nmax_ready, 1)
                    dve.wait_ge(exp_done, 2 * a + 2)
                    dve.reciprocal(rsum[:, a, :], esum[:, a, :]).then_inc(rsum_ready, 1)
                    dve.wait_ge(rsum_ready, a + 1)
                    for t in range(T):
                        dve.tensor_scalar(prob[:, a % 2, t, :], prob[:, a % 2, t, :], rsum[:, a, t:t + 1],
                                          None, ALU.mult).then_inc(prob_ready, 1)
                a = g - A_PV - 2
                if 0 <= a < HEADS:
                    dve.wait_ge(o_hi, a + 1)
                    tile = (a + NAH) % KT
                    dve.scalar_tensor_tensor(out=oT[:, tile, S:2 * S],
                                             in0=ps[:, 6, 0:S],
                                             scalar=par[:, NAG + tile:NAG + tile + 1],
                                             in1=oT[:, tile, 0:S].bitcast(F32), op0=ALU.mult,
                                             op1=ALU.subtract).then_inc(o_lo, 1)
                for i, last in ((0, GH), (1, HEADS)):
                    if g == A_SUMSQ + last - 1 + 2:
                        dve.wait_ge(head_summed, last)
                        dve.tensor_reduce(ssqo[:, i, :],
                                          headsq_ps[:, last - 8:last, :].rearrange("p a t -> p t a"),
                                          AX.X, ALU.add).then_inc(osum_ready, 1)
                        dve.wait_ge(ostd_ready, i + 1)
                        dve.reciprocal(rso[:, i, :], stdo[:, i, :]).then_inc(ors_ready, 1)
                c = (g - G_OUT - 3) // 2
                if (g - G_OUT - 3) % 2 == 0 and 0 <= c < 8:
                    dve.wait_ge(granule_used, g - 1)
                    dve.wait_ge(ors_ready, c // 4 + 1)
                    b = 2 * ((C_OUT + c) % 2)
                    cs = slice(512 * (c % 4), 512 * (c % 4) + 512)
                    if c >= 4:
                        dve.wait_ge(banks_free, C_OUT + c - 3)
                    for t in range(T):
                        ins = dve.scalar_tensor_tensor(out=res[:, t, cs], in0=ps[:, b + t, :],
                                                       scalar=rso[:, c // 4, t:t + 1], in1=res[:, t, cs],
                                                       op0=ALU.mult, op1=ALU.add)
                    ins.then_inc(banks_free, 1)
                if g == 46:
                    for e in (0, S + 1):
                        dve.memset(u[:, :, :, e:e + 1], 0.0).then_inc(pads_zero, 1)
            dve.wait_ge(squared, T + 8)
            dve.tensor_reduce(ssq2, ssq2p, AX.X, ALU.add).then_inc(stat_ready, 1)
            dve.wait_ge(std_ready, 2)
            dve.reciprocal(rs2, std2).then_inc(stat_ready, 1)
            dve.wait_ge(stat_ready, 3)
            for t in range(T):
                dve.tensor_scalar(h2n[:, t, :], res[:, t, :], rs2[:, t:t + 1], None, ALU.mult)\
                    .then_inc(normed, 1)
            turned_lo(h2T, LN2, KT)
            split_at(G_UP + 2)
            dve.wait_ge(pads_zero, 2)

            with dve.Fori(0, UPC) as c:
                for j in range(4):
                    g = G_UP + 3 + j
                    split_lo(g % RAW, g % HIS, c * 4 + (g + 1))
                    half = j // 2
                    if j % 2 == 0:
                        b = 2 * ((C_UP + half) % 2)
                        dve.wait_ge(cross_copied, c * 2 + (8 + half + 1))
                        dve.wait_ge(banks_free, c * 2 + (C_UP + half))
                        dve.tensor_tensor(u[:, half, :, 1:S + 1], ps[:, b:b + 2, 0:S], cross[:, :, :],
                                          ALU.add).then_inc(banks_free, 1)
                        continue
                    dve.wait_ge(centre_ready, c * 4 + (2 * half + 2))
                    for f in range(2):
                        col = c * 2 + (CONV + half * FT + f)
                        dve.scalar_tensor_tensor(out=y[:, half, f, :], in0=u[:, half, f, 0:S],
                                                 scalar=par[:, bass.ds(col, 1)], in1=y[:, half, f, :],
                                                 op0=ALU.mult, op1=ALU.add).then_inc(tap_done, 1)
                    for f in range(2):
                        dve.wait_ge(tap_done, c * 4 + (2 * half + f + 1))
                        col = c * 2 + (CONV + 4 * FT + half * FT + f)
                        dve.scalar_tensor_tensor(out=y[:, half, f, :], in0=u[:, half, f, 2:S + 2],
                                                 scalar=par[:, bass.ds(col, 1)], in1=y[:, half, f, :],
                                                 op0=ALU.mult, op1=ALU.add).then_inc(conv_ready, 1)
                    if half == 0:
                        continue
                    dve.wait_ge(silu_ready, c + 1)
                    dve.wait_ge(conv_ready, c * 4 + 4)
                    dve.tensor_tensor(prod[:, :, :], y[:, 0], y[:, 1], ALU.mult).then_inc(prod_ready, 1)
                    dve.wait_ge(act_hi, c + 1)
                    tiles = bass.ds(c * 2, 2)
                    dve.tensor_tensor(actT[:, tiles, S:2 * S], prod[:, :, :],
                                      actT[:, tiles, 0:S].bitcast(F32), ALU.subtract).then_inc(act_lo, 1)
            split_at(G_DOWN + 3)
            with dve.Fori(0, DNB - 1) as b:
                for j in range(4):
                    g = G_DOWN + 4 + j
                    split_lo(g % RAW, g % HIS, b * 4 + (g + 1))
            for t in range(T):
                for cb in range(4):
                    dve.wait_ge(granule_used, G_END)
                    cs = slice(512 * cb, 512 * cb + 512)
                    dve.tensor_tensor(res[:, t, cs], ps[:, (4 + 2 * cb + t) % 8, :], res[:, t, cs], ALU.add)\
                        .then_inc(x2_ready, 1)
            dve.wait_ge(std_ready, 3)
            dve.reciprocal(rs3, std3).then_inc(stat_ready, 1)
            dve.wait_ge(stat_ready, 4)
            dve.wait_ge(fgain_loaded, 16)
            for t in range(T):
                dve.scalar_tensor_tensor(out=res[:, t, :], in0=res[:, t, :], scalar=rs3[:, t:t + 1],
                                         in1=fgain[:, :], op0=ALU.mult, op1=ALU.mult).then_inc(y_ready, 1)

        @block.tensor
        def _(pe):
            def turn_tiles(src, n0):
                for k in range(KT):
                    if k >= 8 and k % 2 == 0:
                        pe.wait_ge(tile_lo, n0 + k - 6)
                    b, h = 4 + (k // 2) % 4, k % 2
                    for t in range(T):
                        mm = pe.transpose(ps[:, b, S * h + P * t:S * h + P * t + P],
                                          src[:, t, P * k:P * k + P], ident[:, :])
                    mm.then_inc(tile_turned, 1)

            def tokens_granule(tok, k0, banks, raw_slot, hi_slot, first, last):
                hi = whi[:, hi_slot, :].rearrange("p (k n) -> p k n", k=4)
                lo = wlo[:, raw_slot, :].rearrange("p (k n) -> p k n", k=4)
                for kk in range(4):
                    k = k0 + kk
                    for t, b in enumerate(banks):
                        o = ps[:, b, :]
                        th, tl = tok[:, k, P * t:P * t + P], tok[:, k, S + P * t:S + P * t + P]
                        pe.matmul(o, th, hi[:, kk, :], start=first and kk == 0, stop=False)
                        pe.matmul(o, th, lo[:, kk, :], start=False, stop=False)
                        mm = pe.matmul(o, tl, hi[:, kk, :], start=False, stop=last and kk == 3)
                mm.then_inc(granule_used, 1)

            def weights_granule(tok, k0, banks, raw_slot, hi_slot):
                hi = whi[:, hi_slot, :].rearrange("p (k n) -> p k n", k=8)
                lo = wlo[:, raw_slot, :].rearrange("p (k n) -> p k n", k=8)
                for f, b in enumerate(banks):
                    for kk in range(8):
                        k = k0 + kk
                        pe.matmul(ps[:, b, :], hi[:, kk, P * f:P * f + P], tok[:, k, :],
                                  start=k == 0, stop=False, skip_group_check=True)
                        mm = pe.matmul(ps[:, b, S:2 * S], lo[:, kk, P * f:P * f + P], tok[:, k, 0:S],
                                       start=False, stop=k == KT - 1, skip_group_check=True)
                mm.then_inc(granule_used, 1)

            pe.wait_ge(ident_ready, 1)
            pe.wait_ge(params_loaded, 16 * 8)
            pe.transpose(ps[:, 0, 0:CONV], stage[0:CONV, 0, :], ident[0:CONV, 0:CONV])
            for j in range(4):
                c0 = CONV + 2 * FT * j
                mm = pe.transpose(ps[:, 0, c0:c0 + 2 * FT], stage[0:2 * FT, 1 + j, :],
                                  ident[0:2 * FT, 0:2 * FT])
            mm.then_inc(par_in_psum, 1)
            pe.wait_ge(normed, T)
            turn_tiles(xn, 0)

            for g in range(G_UP):
                pe.wait_ge(lo_ready, g + 1)
                if g < G_NAQK:
                    chunk, kq = divmod(g, 4)
                    if chunk == 0:
                        pe.wait_ge(tile_lo, 4 * kq + 4)
                    if kq == 0 and chunk >= 2:
                        pe.wait_ge(banks_free, chunk - 1)
                    b = 2 * (chunk % 2)
                    tokens_granule(xT, 4 * kq, (b, b + 1), g % RAW, g % HIS, kq == 0, kq == 3)
                elif g < G_OUT:
                    c, kh = divmod(g - G_NAQK, 2)
                    chunk = 5 + c
                    if kh == 0:
                        pe.wait_ge(banks_free, chunk - 1)
                    b = 2 * (chunk % 2)
                    weights_granule(xT, 8 * kh, (b, b + 1), g % RAW, g % HIS)
                else:
                    c, kh = divmod(g - G_OUT, 2)
                    chunk = C_OUT + c
                    if kh == 0:
                        pe.wait_ge(banks_free, chunk - 1)
                    if c in (0, 4):
                        pe.wait_ge(o_lo, GH if c == 0 else HEADS)
                    b = 2 * (chunk % 2)
                    tokens_granule(oT, (NAH if c < 4 else 0) + 4 * kh, (b, b + 1), g % RAW, g % HIS,
                                   kh == 0, kh == 1)

                if 20 <= g < 25:
                    i = g - 20
                    if i == 0:
                        pe.wait_ge(rope_step, 21)
                    else:
                        pe.wait_ge(g_copied, i)
                    h0 = (2 * (i - 1)) % 10
                    for h in range(2):
                        for t in range(T):
                            mm = pe.transpose(ps[:, 7, S * h + P * t:S * h + P * t + P],
                                              gproj[:, t, DH * (h0 + h):DH * (h0 + h) + DH], ident[:, :])
                    mm.then_inc(g_turned, 1)
                a = g - A_SCORES
                if 0 <= a < HEADS:
                    if a < GH:
                        pe.wait_ge(g_copied, 2 + a // 2)
                        q, k = gT[:, a, :], gT[:, GH + a // (GH // GKV), :]
                    else:
                        n = a - GH
                        pe.wait_ge(banks_free, 7 + 2 * (n // 2))
                        i = 4 * (n // 2) + n % 2
                        q, k = naqkT[:, i, :], naqkT[:, i + 2, :]
                    if a >= 1:
                        pe.wait_ge(exp_done, 2 * a)
                    for t in range(T):
                        mm = pe.matmul(scores_ps[:, t, :], q[:, P * t:P * t + P], k, start=True, stop=True)
                    mm.then_inc(scored, 1)
                a = g - A_TRANSPOSE
                if 0 <= a < HEADS:
                    pe.wait_ge(prob_ready, 2 * a + 2)
                    if a >= 1:
                        pe.wait_ge(probT_ready, a)
                    for k in range(T):
                        for t in range(T):
                            mm = pe.transpose(probT_ps[:, k, P * t:P * t + P],
                                              prob[:, a % 2, t, P * k:P * k + P], ident[:, :])
                    mm.then_inc(prob_turned, 1)
                a = g - A_PV
                if 0 <= a < HEADS:
                    pe.wait_ge(probT_ready, a + 1)
                    if a >= 1:
                        pe.wait_ge(o_lo, a)
                    for k in range(T):
                        if a < GH:
                            v0 = (GH + GKV + a // (GH // GKV)) * DH
                            v = gproj[:, k, v0:v0 + DH]
                        else:
                            v = nav[:, k, DH * (a - GH):DH * (a - GH) + DH]
                        mm = pe.matmul(ps[:, 6, 0:S], v, probT[:, a % 2, k, :],
                                       start=k == 0, stop=k == T - 1)
                    mm.then_inc(pv_done, 1)
                a = g - A_SUMSQ
                if 0 <= a < HEADS:
                    pe.wait_ge(osq_ready, a + 1)
                    if a == 0:
                        pe.wait_ge(ones_ready, 1)
                        pe.wait_ge(g_copied, 5)
                    if a == GH:
                        pe.wait_ge(osum_ready, 1)
                    for t in range(T):
                        mm = pe.matmul(headsq_ps[:, a, t:t + 1], osq[:, a % 2, P * t:P * t + P], ones[:, :],
                                       start=True, stop=True)
                    mm.then_inc(head_summed, 1)

            pe.wait_ge(normed, 2 * T)
            turn_tiles(h2n, KT)
            pe.wait_ge(tile_lo, 2 * KT)
            with pe.Fori(0, UPC) as c:
                for j in range(4):
                    g = G_UP + j
                    pe.wait_ge(lo_ready, c * 4 + (g + 1))
                    chunk = C_UP + j // 2
                    if j % 2 == 0:
                        pe.wait_ge(banks_free, c * 2 + (chunk - 1))
                    b = 2 * (chunk % 2)
                    weights_granule(h2T, 8 * (j % 2), (b, b + 1), g % RAW, g % HIS)

            for n in range(4 * DNB):
                blk, cb = divmod(n, 4)
                g = G_DOWN + n
                pe.wait_ge(lo_ready, g + 1)
                if cb == 0:
                    pe.wait_ge(act_lo, 2 * blk + 2)
                if n == 2:
                    pe.wait_ge(banks_free, C_UP + 2 * UPC)
                b = (4 + 2 * cb) % 8
                tokens_granule(actT, 4 * blk, (b, b + 1), g % RAW, g % HIS, blk == 0, blk == DNB - 1)


_INS = ["x", "ln1_g", "w_in", "na_rpb", "q_norm_g", "k_norm_g", "na_out_g", "gqa_out_g", "w_out",
        "ln2_g", "w_up", "conv_w", "conv_b", "w_down", "final_g"]


def kernel(**inputs):
    import numpy as _np
    import concourse.bacc as _bacc
    from concourse import mybir as _mybir
    from concourse.bass_utils import run_bass_kernel_spmd as _run

    nc = _bacc.Bacc("TRN2", target_bir_lowering=False, num_devices=1)
    arrays, args = {}, []

    def give(name, a):
        arrays[f"in_{name}_dram"] = a
        args.append(nc.dram_tensor(f"in_{name}_dram", a.shape, _mybir.dt.from_np(a.dtype),
                                   kind="ExternalInput").ap())

    for name in _INS:
        a = _np.asarray(inputs[name])
        if name == "na_rpb":
            a = a[..., ::-1]
        give(name, _np.ascontiguousarray(a))
    t = _np.arange(S)
    inv = (1.0 / (10000.0 ** (_np.arange(0, DH // 2, 2, dtype=_np.float32) / (DH // 2)))).astype(_np.float32)
    ang = _np.concatenate([(t // GW).astype(_np.float32)[:, None] * inv,
                           (t % GW).astype(_np.float32)[:, None] * inv], axis=-1)
    give("cos", _np.repeat(_np.cos(ang), 2, axis=-1).astype(_np.float32))
    give("sin", _np.stack([-_np.sin(ang), _np.sin(ang)], axis=-1).reshape(S, DH).astype(_np.float32))
    args.append(nc.dram_tensor("out_0_dram", (1, S, D), F32, kind="ExternalOutput").ap())
    hybrid_block(nc, *args)
    r = _run(nc, [arrays], core_ids=[0])
    return r.results[0]["out_0_dram"]
```

```python
from contextlib import ExitStack

import concourse.bass as bass
from concourse import mybir
from concourse.alu_op_type import AluOpType as ALU

ACT = mybir.ActivationFunctionType
AX = mybir.AxisListType
F32 = mybir.dt.float32
F32R = mybir.dt.float32r

P = 128
D = 2048
S = 256
T = S // P
KT = D // P
DH = 128
NAH = 8
GH = 8
GKV = 2
GW = 64
ROWS = S // GW
RPB_R, RPB_C = 15, 31
FF = 5632
FT = FF // P
EPS = 1e-6
SCALE = float(DH) ** -0.5
MASKED = -1.0e30

RAW = 4
HIS = 2
G_GQA = 0
G_NAV = G_GQA + 12
G_NAQK = G_NAV + 8
G_OUT = G_NAQK + 16
G_UP = G_OUT + 16
UPC = FF // 256
G_DOWN = G_UP + 4 * UPC
DNB = FT // 4
DROW = 8
G_END = G_DOWN + 4 * DNB

C_OUT = 13
C_UP = C_OUT + 8

A_SCORES = 23
A_TRANSPOSE = A_SCORES + 2
A_PV = A_SCORES + 3
A_SUMSQ = A_SCORES + 4
HEADS = GH + NAH

DOWN = [(b, cb) for b in range(DROW) for cb in range(4)] + \
       [(b, cb) for cb in range(4) for b in range(DROW, DNB)]

LN1, LN2, NAG, GQAG = 0, KT, 2 * KT, 2 * KT + NAH
CONV = 2 * KT + NAH + GH
PARAMS = CONV + 4 * 2 * FT


def hybrid_block(nc, x, ln1_g, w_in, na_rpb, q_norm_g, k_norm_g, na_out_g, gqa_out_g, w_out,
                 ln2_g, w_up, conv_w, conv_b, w_down, final_g, cos_t, sin_t, out):
    with ExitStack() as ctx:
        sem = lambda name: ctx.enter_context(nc.semaphore(name))

        BASE = 16512
        A_RES = BASE
        A_X = A_RES + T * D * 4
        A_E = A_X + KT * 2 * S * 4
        A_O = A_E + 57344
        A_RAW = A_O + KT * 2 * S * 4
        A_HI = A_RAW + RAW * 8192
        A_M = A_HI + HIS * 8192

        def at(name, shape, dt, offset):
            return nc.alloc_sbuf_tensor_at(name, shape, dt, offset=offset)

        res = at("res", [P, T, D], F32, A_RES)
        xT = at("xT", [P, KT, 2 * S], F32R, A_X)
        naqkT = at("naqkT", [P, 2 * NAH, S], F32, A_E)
        nav = at("nav", [P, T, NAH * DH], F32, A_E + 16384)
        gproj = at("gproj", [P, T, 1536], F32, A_E + 24576)
        gT = at("gT", [P, GH + GKV, S], F32, A_E + 36864)
        prob = at("prob", [P, 2, T, S], F32, A_E + 47104)
        probT = at("probT", [P, 2, T, S], F32, A_E + 51200)
        osq = at("osq", [P, S], F32, A_E + 55296)
        rms1 = at("rms1", [P, S], F32, A_E + 56320)
        oT = at("oT", [P, KT, 2 * S], F32R, A_O)
        h2T = at("h2T", [P, KT, 2 * S], F32R, A_X)
        junk1 = at("junk1", [P, T, D], F32, A_O)
        junk2 = at("junk2", [P, T, D], F32, A_E)
        stage = at("stage", [P, 5, P], F32, A_O + 16384)
        rot_n = at("rot_n", [P, 10, DH], F32, A_O + 16384)
        rot_m = at("rot_m", [P, 10, DH], F32, A_O + 16384 + 5120)
        diag1 = at("diag1", [P, T, P], F32, A_O + 29696)
        cosr = at("cosr", [P, T, DH], F32, A_O + 26624)
        sinr = at("sinr", [P, T, DH], F32, A_O + 27648)
        grow = at("grow", [P, 2, DH], F32, A_O + 28672)
        actT = at("actT", [P, FT, 2 * S], F32R, A_E)
        fgain = at("fgain", [P, D], F32, A_X)
        yout = at("yout", [P, T, D], F32, A_X + 8192)
        junk3 = at("junk3", [P, T, 512], F32, A_X + 24576)
        raw = at("raw", [P, RAW, 2048], F32, A_RAW)
        wlo = at("wlo", [P, RAW, 2048], F32R, A_RAW)
        whi = at("whi", [P, HIS, 2048], F32R, A_HI)
        par = at("par", [P, PARAMS], F32, A_M)
        stat = at("stat", [P, 256], F32, A_M + 1600)
        ident = at("ident", [P, P], F32, A_M + 2624)
        eps = at("eps", [P, 1], F32, A_M + 3136)
        ones = at("ones", [P, P], F32, A_M + 3168)
        A_W = A_M + 3680
        bias = at("bias", [P, NAH, 6, GW], F32, A_W)
        u = at("u", [P, 2, 2, S + 2], F32, A_W)
        y = at("y", [P, 2, 2, S], F32, A_W + 4160)
        prod = at("prod", [P, 2, S], F32, A_W + 8256)
        rms2 = at("rms2", [P, S], F32, A_W + 10304)
        diag2 = at("diag2", [P, T, P], F32, A_W + 16384)
        cosg = at("cosg", [P, T, 2, DH], F32, A_W + 12288)
        sing = at("sing", [P, T, 2, DH], F32, A_W + 14336)
        biased = at("biased", [P, T, S], F32, A_W + 16384)
        cross = at("cross", [P, 2, S], F32, A_W + 18432)

        ps = ctx.enter_context(nc.psum_tensor("ps", [P, 8, 512], F32))
        scores_ps = ps[:, 4, :].rearrange("p (t k) -> p t k", t=T)
        probT_ps = ps[:, 5, :].rearrange("p (k q) -> p k q", k=T)

        ssq1, std1, rs1 = stat[:, 0:2], stat[:, 2:4], stat[:, 4:6]
        ssq2p = stat[:, 8:16].rearrange("p (t c) -> p t c", t=T)
        ssq2, std2, rs2 = stat[:, 16:18], stat[:, 18:20], stat[:, 20:22]
        ssq3, std3, rs3 = stat[:, 24:26], stat[:, 26:28], stat[:, 28:30]
        ssq3p = stat[:, 240:248].rearrange("p (t c) -> p t c", t=T)
        ssqg = stat[:, 32:52].rearrange("p (t h) -> p t h", t=T)
        stdg = stat[:, 52:72].rearrange("p (t h) -> p t h", t=T)
        rsg = stat[:, 72:92].rearrange("p (t h) -> p t h", t=T)
        ssqo = stat[:, 96:100].rearrange("p (g t) -> p g t", g=2)
        stdo = stat[:, 100:104].rearrange("p (g t) -> p g t", g=2)
        rso = stat[:, 104:108].rearrange("p (g t) -> p g t", g=2)
        smax = stat[:, 112:144].rearrange("p (a t) -> p a t", t=T)
        nmax = stat[:, 144:176].rearrange("p (a t) -> p a t", t=T)
        esum = stat[:, 176:208].rearrange("p (a t) -> p a t", t=T)
        rsum = stat[:, 208:240].rearrange("p (a t) -> p a t", t=T)
        headsq_ps = ps[:, 7, 0:2 * HEADS].rearrange("p (a t) -> p a t", t=T)

        x_loaded = [sem(f"x_loaded{h}") for h in range(2)]
        gains_loaded, conv_loaded = sem("gains_loaded"), sem("conv_loaded")
        rope_loaded = sem("rope_loaded")
        bias_loaded = sem("bias_loaded")
        fgain_loaded = sem("fgain_loaded")
        stored = sem("stored")
        w_loaded = [sem(f"w_loaded{i}") for i in range(RAW)]
        hi_ready = sem("hi_ready")
        lo_ready = sem("lo_ready")
        granule_used = sem("granule_used")
        banks_free = sem("banks_free")
        ident_zero, ident_ready = sem("ident_zero"), sem("ident_ready")
        ones_ready, eps_ready = sem("ones_ready"), sem("eps_ready")
        bias_masked = sem("bias_masked")
        par_in_psum, par_ready = sem("par_in_psum"), sem("par_ready")
        squared, std_ready, stat_ready = sem("squared"), sem("std_ready"), sem("stat_ready")
        diag_ready, rms_spread, rms_ready = sem("diag_ready"), sem("rms_spread"), sem("rms_ready")
        tile_turned = sem("tile_turned")
        tile_hi, tile_lo = sem("tile_hi"), sem("tile_lo")
        cross_copied = sem("cross_copied")
        tables_ready = sem("tables_ready")
        rope_step = sem("rope_step")
        stdg_ready = sem("stdg_ready")
        g_turned, g_copied = sem("g_turned"), sem("g_copied")
        scored = sem("scored")
        biased_ready = sem("biased_ready")
        max_ready, nmax_ready = sem("max_ready"), sem("nmax_ready")
        exp_done = sem("exp_done")
        rsum_ready, prob_ready = sem("rsum_ready"), sem("prob_ready")
        prob_turned, probT_ready = sem("prob_turned"), sem("probT_ready")
        pv_done = sem("pv_done")
        osq_ready, o_hi, o_lo = sem("osq_ready"), sem("o_hi"), sem("o_lo")
        head_summed = sem("head_summed")
        osum_ready, ostd_ready, ors_ready = sem("osum_ready"), sem("ostd_ready"), sem("ors_ready")
        pads_zero = sem("pads_zero")
        u_ready, centre_ready = sem("u_ready"), sem("centre_ready")
        qk_summed = sem("qk_summed")
        tap_done, conv_ready = sem("tap_done"), sem("conv_ready")
        silu_ready, prod_ready = sem("silu_ready"), sem("prod_ready")
        act_hi, act_lo = sem("act_hi"), sem("act_lo")
        x2_ready, gained = sem("x2_ready"), sem("gained")
        y_ready = [sem(f"y_ready{t}") for t in range(T)]

        w_in_v = w_in[0].rearrange("(k p) n -> p k n", p=P)
        w_out_v = w_out[0].rearrange("(k p) n -> p k n", p=P)
        w_up_v = w_up[0].rearrange("(k p) n -> p k n", p=P)
        w_down_v = w_down[0].rearrange("(b k p) n -> b p k n", p=P, k=4)
        NA_W = NAH * DH

        def source(g):
            if g < G_NAQK:
                c, kq = divmod(g, 4)
                col = 3 * NA_W + 512 * c if c < 3 else 2 * NA_W + 512 * (c - 3)
                return w_in_v[:, 4 * kq:4 * kq + 4, col:col + 512]
            if g < G_OUT:
                c, kh = divmod(g - G_NAQK, 2)
                col = (c % 2) * NA_W + 256 * (c // 2)
                return w_in_v[:, 8 * kh:8 * kh + 8, col:col + 256]
            c, kh = divmod(g - G_OUT, 2)
            k = (NAH if c < 4 else 0) + 4 * kh
            return w_out_v[:, k:k + 4, 512 * (c % 4):512 * (c % 4) + 512]

        block = ctx.enter_context(nc.Block())

        @block.sync
        def _(sp):
            xv = x[0].rearrange("(t p) d -> p t d", p=P)
            for h in range(2):
                cs = slice(h * D // 2, (h + 1) * D // 2)
                sp.dma_start(res[:, :, cs], xv[:, :, cs]).then_inc(x_loaded[h], 16)

            def load(slot, src):
                k = src.shape[1]
                dst = raw[:, slot, :].rearrange("p (k n) -> p k n", k=k)
                sp.dma_start(dst, src).then_inc(w_loaded[slot], 16)

            for g in range(G_UP):
                if g >= RAW:
                    sp.wait_ge(granule_used, g - RAW + 1)
                load(g % RAW, source(g))
            with sp.Fori(0, UPC) as c:
                for j in range(4):
                    sp.wait_ge(granule_used, c * 4 + (G_UP + j - RAW + 1))
                    col = c * 256 + (j // 2) * FF
                    load((G_UP + j) % RAW, w_up_v[:, 8 * (j % 2):8 * (j % 2) + 8, bass.ds(col, 256)])
            with sp.Fori(0, DROW) as b:
                for j in range(4):
                    sp.wait_ge(granule_used, b * 4 + (G_DOWN + j - RAW + 1))
                    src = w_down_v[bass.ds(b, 1), :, :, 512 * j:512 * j + 512].rearrange(
                        "o p k n -> (o p) k n")
                    load((G_DOWN + j) % RAW, src)
            sp.dma_start(fgain[:, :], final_g.rearrange("(o d) -> o d", o=1).broadcast_to([P, D]))\
                .then_inc(fgain_loaded, 16)
            for n in range(4 * DROW, 4 * DNB):
                b, cb = DOWN[n]
                sp.wait_ge(granule_used, G_DOWN + n - RAW + 1)
                load((G_DOWN + n) % RAW, w_down_v[b, :, :, 512 * cb:512 * cb + 512])
            ov = out[0].rearrange("(t p) d -> p t d", p=P)
            for h in range(2):
                for t in range(T):
                    sp.wait_ge(y_ready[t], h + 1)
                    cs = slice(h * D // 2, (h + 1) * D // 2)
                    sp.dma_start(ov[:, t, cs], yout[:, t, cs]).then_inc(stored, 16)
            sp.wait_ge(stored, 16 * 2 * T)

        @block.gpsimd
        def _(pool):
            pool.memset(ones[:, :], 1.0).then_inc(ones_ready, 1)
            pool.memset(ident[:, :], 0.0).then_inc(ident_zero, 1)
            pool.wait_ge(ident_zero, 1)
            pool.affine_select(out=ident[:, :], in_=ident[:, :], compare_op=ALU.not_equal, fill=1.0,
                               base=0, pattern=[[-1, P]], channel_multiplier=1).then_inc(ident_ready, 1)
            pool.wait_ge(bias_loaded, 16 * 2 * NAH)
            n = 0
            for half in range(2):
                b = bias[GW * half:GW * half + GW].rearrange("p h j m -> p (h j) m")
                left, right = b[:, :, 16:64], b[:, :, 0:48]
                pool.affine_select(out=left, in_=left, compare_op=ALU.is_ge, fill=MASKED, base=55,
                                   pattern=[[0, 6 * NAH], [-1, 48]], channel_multiplier=-1)\
                    .then_inc(bias_masked, 1)
                n += 1
                pool.wait_ge(bias_masked, n)
                pool.affine_select(out=right, in_=right, compare_op=ALU.is_ge, fill=MASKED, base=-56,
                                   pattern=[[0, 6 * NAH], [1, 48]], channel_multiplier=1)\
                    .then_inc(bias_masked, 1)
                n += 1

        @block.scalar
        def _(act):
            row = 0
            for vec, rows in ((ln1_g, KT), (ln2_g, KT), (na_out_g, NAH), (gqa_out_g, GH)):
                act.dma_start(stage[row:row + rows, 0, :], vec[0].rearrange("(f p) -> f p", p=P))\
                    .then_inc(gains_loaded, 16)
                row += rows
            for j in range(4):
                vec = conv_w[0, j, :] if j < 3 else conv_b[0]
                act.dma_start(stage[0:2 * FT, 1 + j, :], vec.rearrange("(f p) -> f p", p=P))\
                    .then_inc(conv_loaded, 16)
            for i, vec in enumerate((q_norm_g, k_norm_g)):
                act.dma_start(grow[:, i, :], vec.broadcast_to([P, DH])).then_inc(rope_loaded, 16)
            act.dma_start(cosr[:, :, :], cos_t.rearrange("(t p) d -> p t d", p=P)).then_inc(rope_loaded, 16)
            act.dma_start(sinr[:, :, :], sin_t.rearrange("(t p) d -> p t d", p=P)).then_inc(rope_loaded, 16)

            def split_hi(slot_raw, slot_hi, loaded, used):
                act.wait_ge(w_loaded[slot_raw], loaded)
                if used is not None:
                    act.wait_ge(granule_used, used)
                act.activation(whi[:, slot_hi, :], raw[:, slot_raw, :], ACT.Copy).then_inc(hi_ready, 1)

            def split_at(g):
                split_hi(g % RAW, g % HIS, 16 * (g // RAW + 1), g - HIS + 1 if g >= HIS else None)

            def turned_hi(dst, gain0, n0, tiles):
                for k in tiles:
                    act.wait_ge(tile_turned, n0 + k + 2 - k % 2)
                    b, h = 4 + (k // 2) % 4, k % 2
                    act.activation(dst[:, k, 0:S], ps[:, b, S * h:S * h + S], ACT.Copy,
                                   scale=par[:, gain0 + k:gain0 + k + 1]).then_inc(tile_hi, 1)

            act.wait_ge(par_ready, 1)
            turned_hi(xT, LN1, 0, range(8))
            split_at(0)
            turned_hi(xT, LN1, 0, range(8, KT))
            for half in range(2):
                for h in range(NAH):
                    off = h * RPB_R * RPB_C + (5 - half) * RPB_C + 15 - (GW - 1)
                    src = bass.AP(na_rpb.tensor, off, [[1, GW], [RPB_C, 6], [1, GW]])
                    act.dma_start(bias[GW * half:GW * half + GW, h], src).then_inc(bias_loaded, 16)

            for g in range(1, G_UP + 2):
                split_at(g)
                if g < 3:
                    t = g - 1
                    act.wait_ge(x_loaded[0], 16)
                    act.wait_ge(x_loaded[1], 16)
                    act.activation(junk1[:, t, :], res[:, t, :], ACT.Square, accum_out=ssq1[:, t:t + 1])\
                        .then_inc(squared, 1)
                if g == 3:
                    act.wait_ge(squared, T)
                    act.wait_ge(eps_ready, 1)
                    act.activation(std1, ssq1, ACT.Sqrt, bias=eps[:, :], scale=1.0 / D).then_inc(std_ready, 1)
                if g == 7:
                    act.wait_ge(rms_spread, 1)
                    act.activation(rms1[:, :], ps[:, 7, 0:S], ACT.Copy).then_inc(rms_ready, 1)
                c = (g - G_NAQK - 3) // 2
                if (g - G_NAQK - 3) % 2 == 0 and 0 <= c < 8:
                    act.wait_ge(granule_used, g - 1)
                    if c >= 1:
                        act.wait_ge(banks_free, 5 + c)
                    b = 2 * ((5 + c) % 2)
                    act.activation(cross[:, :, :], ps[:, b:b + 2, S:2 * S], ACT.Copy).then_inc(cross_copied, 1)
                if g == 15:
                    act.wait_ge(rope_step, 4)
                    act.activation(stdg, ssqg, ACT.Sqrt, bias=eps[:, :], scale=1.0 / DH).then_inc(stdg_ready, 1)
                if 22 <= g < 27:
                    i = g - 22
                    act.wait_ge(g_turned, i + 1)
                    h0 = (2 * (i - 1)) % 10
                    act.activation(gT[:, h0:h0 + 2, :], ps[:, 7, :].rearrange("p (h s) -> p h s", h=2),
                                   ACT.Copy).then_inc(g_copied, 1)
                a = g - A_SCORES - 2
                if 0 <= a < HEADS:
                    act.wait_ge(nmax_ready, a + 1)
                    if a >= 2:
                        act.wait_ge(prob_turned, a - 1)
                    for t in range(T):
                        src, sc = (scores_ps, SCALE) if a < GH else (biased, 1.0)
                        act.activation(prob[:, a % 2, t, :], src[:, t, :], ACT.Exp, bias=nmax[:, a, t:t + 1],
                                       scale=sc, accum_out=esum[:, a, t:t + 1]).then_inc(exp_done, 1)
                a = g - A_TRANSPOSE - 2
                if 0 <= a < HEADS:
                    act.wait_ge(prob_turned, a + 1)
                    if a >= 2:
                        act.wait_ge(pv_done, a - 1)
                    act.activation(probT[:, a % 2], probT_ps, ACT.Copy).then_inc(probT_ready, 1)
                a = g - A_PV - 2
                if 0 <= a < HEADS:
                    act.wait_ge(pv_done, a + 1)
                    if a >= 1:
                        act.wait_ge(head_summed, a)
                    o = ps[:, 6, 0:S]
                    act.activation(osq[:, :], o, ACT.Square).then_inc(osq_ready, 1)
                    tile = (a + NAH) % KT
                    act.activation(oT[:, tile, 0:S], o, ACT.Copy, scale=par[:, NAG + tile:NAG + tile + 1])\
                        .then_inc(o_hi, 1)
                for i, last in ((0, GH), (1, HEADS)):
                    if g == A_SUMSQ + last - 1 + 2:
                        act.wait_ge(osum_ready, i + 1)
                        act.activation(stdo[:, i, :], ssqo[:, i, :], ACT.Sqrt, bias=eps[:, :],
                                       scale=1.0 / (NAH * DH)).then_inc(ostd_ready, 1)
                c = (g - G_OUT - 3) // 2
                if (g - G_OUT - 3) % 2 == 0 and 4 <= c < 8:
                    act.wait_ge(banks_free, C_OUT + c + 1)
                    for t in range(T):
                        cs = slice(512 * (c - 4), 512 * (c - 4) + 512)
                        act.activation(junk2[:, t, cs], res[:, t, cs], ACT.Square,
                                       accum_out=ssq2p[:, t, c - 4:c - 3]).then_inc(squared, 1)
                    turned_hi(h2T, LN2, KT, range(4 * (c - 4), 4 * (c - 3)))
            act.wait_ge(stat_ready, 2)
            act.activation(std2, ssq2, ACT.Sqrt, bias=eps[:, :], scale=1.0 / D).then_inc(std_ready, 1)
            act.preload_act_table(ACT.Silu)
            split_at(G_UP + 2)
            act.wait_ge(rms_spread, 2)
            act.activation(rms2[:, :], ps[:, 7, 0:S], ACT.Copy).then_inc(rms_ready, 1)

            def act_high(c):
                act.wait_ge(prod_ready, c + 1)
                act.activation(actT[:, bass.ds(c * 2, 2), 0:S], prod[:, :, :], ACT.Copy).then_inc(act_hi, 1)

            def up_chunk(c, first):
                for j in range(4):
                    g = G_UP + 3 + j
                    split_hi(g % RAW, g % HIS, c * 16 + 16 * (g // RAW + 1), c * 4 + (g - HIS + 1))
                    half = j // 2
                    if j % 2 == 0:
                        b = 2 * ((C_UP + half) % 2)
                        act.wait_ge(granule_used, c * 4 + (G_UP + 2 * half + 2))
                        act.wait_ge(banks_free, c * 2 + (C_UP + half))
                        act.activation(cross[:, :, :], ps[:, b:b + 2, S:2 * S], ACT.Copy)\
                            .then_inc(cross_copied, 1)
                        if half == 0 and not first:
                            act_high(c - 1)
                        if half == 1:
                            act.wait_ge(conv_ready, c * 4 + 2)
                            act.activation(y[:, 0], y[:, 0], ACT.Silu).then_inc(silu_ready, 1)
                        continue
                    act.wait_ge(u_ready, c * 2 + (half + 1))
                    for f in range(2):
                        col = c * 2 + (CONV + 2 * FT + half * FT + f)
                        act.activation(y[:, half, f, :], u[:, half, f, 1:S + 1], ACT.Identity,
                                       scale=par[:, bass.ds(col, 1)],
                                       bias=par[:, bass.ds(col + 2 * 2 * FT, 1)]).then_inc(centre_ready, 1)

            up_chunk(0, True)
            with act.Fori(1, UPC) as c:
                up_chunk(c, False)
            act_high(UPC - 1)
            split_at(G_DOWN + 3)
            with act.Fori(0, DROW) as b:
                for j in range(4):
                    g = G_DOWN + 4 + j
                    split_hi(g % RAW, g % HIS, b * 16 + 16 * (g // RAW + 1), b * 4 + (g - HIS + 1))

            def out_squares(cb):
                for t in range(T):
                    act.wait_ge(x2_ready, 2 * cb + t + 1)
                    act.activation(junk3[:, t, :], res[:, t, 512 * cb:512 * cb + 512], ACT.Square,
                                   accum_out=ssq3p[:, t, cb:cb + 1]).then_inc(squared, 1)

            for n in range(4 * DROW + 4, 4 * DNB):
                split_at(G_DOWN + n)
                if (n - 4 * DROW - 4) % 3 == 0:
                    cb = (n - 4 * DROW - 4) // 3
                    if cb >= 1:
                        act.wait_ge(squared, T + 8 + 2 * cb)
                    out_squares(cb)
            act.wait_ge(squared, T + 8 + 6)
            out_squares(3)
            act.wait_ge(stat_ready, 4)
            act.activation(std3, ssq3, ACT.Sqrt, bias=eps[:, :], scale=1.0 / D).then_inc(std_ready, 1)
            act.wait_ge(stat_ready, 5)
            act.wait_ge(gained, 8)
            for h in range(2):
                cs = slice(h * D // 2, (h + 1) * D // 2)
                act.activation(yout[:, 1, cs], yout[:, 1, cs], ACT.Copy, scale=rs3[:, 1:2])\
                    .then_inc(y_ready[1], 1)

        @block.vector
        def _(dve):
            dve.memset(eps[:, :], EPS).then_inc(eps_ready, 1)
            def split_lo(slot_raw, slot_hi, ready):
                dve.wait_ge(hi_ready, ready)
                dve.tensor_tensor(wlo[:, slot_raw, :], raw[:, slot_raw, :], whi[:, slot_hi, :].bitcast(F32),
                                  ALU.subtract).then_inc(lo_ready, 1)

            def split_at(g):
                split_lo(g % RAW, g % HIS, g + 1)

            def turned_lo(dst, gain0, n0, tiles):
                for k in tiles:
                    dve.wait_ge(tile_hi, n0 + k + 2 - k % 2)
                    b, h = 4 + (k // 2) % 4, k % 2
                    dve.scalar_tensor_tensor(out=dst[:, k, S:2 * S], in0=ps[:, b, S * h:S * h + S],
                                             scalar=par[:, gain0 + k:gain0 + k + 1],
                                             in1=dst[:, k, 0:S].bitcast(F32), op0=ALU.mult,
                                             op1=ALU.subtract).then_inc(tile_lo, 1)

            def diagonal(dst, rs):
                for t in range(T):
                    ins = dve.tensor_scalar(dst[:, t, :], ident[:, :], rs[:, t:t + 1], None, ALU.mult)
                ins.then_inc(diag_ready, 1)

            dve.wait_ge(par_in_psum, 1)
            dve.tensor_copy(par[:, 0:CONV], ps[:, 0, 0:CONV]).then_inc(par_ready, 1)
            turned_lo(xT, LN1, 0, range(8))
            split_at(0)
            turned_lo(xT, LN1, 0, range(8, KT))

            dve.wait_ge(rope_loaded, 64)
            for t in range(T):
                for i in range(2):
                    dve.tensor_tensor(cosg[:, t, i, :], cosr[:, t, :], grow[:, i, :], ALU.mult)\
                        .then_inc(tables_ready, 1)
                    for e in range(2):
                        dve.tensor_tensor(sing[:, t, i, e::2], sinr[:, t, e::2], grow[:, i, 1 - e::2],
                                          ALU.mult).then_inc(tables_ready, 1)

            def over_heads(table, n):
                return table.unsqueeze(1).broadcast_to([P, n, table.shape[1]])

            groups = ((0, 0, GH), (1, GH, GKV))

            def rope(step, t):
                heads = gproj[:, t, 0:10 * DH].rearrange("p (h d) -> p h d", d=DH)
                if step == 0:
                    if t == 1:
                        dve.wait_ge(rope_step, 2)
                    dve.tensor_tensor(rot_n[:, :, :], heads, heads, ALU.mult).then_inc(rope_step, 1)
                    dve.wait_ge(rope_step, 2 * t + 1)
                    dve.tensor_reduce(ssqg[:, t, :], rot_n[:, :, :], AX.X, ALU.add).then_inc(rope_step, 1)
                if step == 1:
                    base = 4 + 7 * t
                    if t == 0:
                        dve.wait_ge(stdg_ready, 1)
                        dve.reciprocal(rsg, stdg).then_inc(rope_step, 1)
                        dve.wait_ge(rope_step, 5)
                        dve.wait_ge(tables_ready, 12)
                    base = 5 + 8 * t
                    dve.wait_ge(rope_step, base)
                    dve.tensor_tensor(rot_n[:, :, :], heads, rsg[:, t, :].unsqueeze(2).broadcast_to([P, 10, DH]),
                                      ALU.mult).then_inc(rope_step, 1)
                    dve.wait_ge(rope_step, base + 1)
                    for i, h0, n in groups:
                        for e in range(2):
                            dve.tensor_tensor(rot_m[:, h0:h0 + n, e::2], rot_n[:, h0:h0 + n, 1 - e::2],
                                              over_heads(sing[:, t, i, e::2], n), ALU.mult)\
                                .then_inc(rope_step, 1)
                if step == 2:
                    base = 5 + 8 * t + 5
                    dve.wait_ge(rope_step, base)
                    for i, h0, n in groups:
                        dve.tensor_tensor(rot_n[:, h0:h0 + n, :], rot_n[:, h0:h0 + n, :],
                                          over_heads(cosg[:, t, i, :], n), ALU.mult).then_inc(rope_step, 1)
                    dve.wait_ge(rope_step, base + 2)
                    dve.tensor_tensor(heads, rot_n[:, :, :], rot_m[:, :, :], ALU.add).then_inc(rope_step, 1)

            for g in range(1, G_UP + 2):
                split_at(g)
                if g == 2:
                    dve.wait_ge(par_in_psum, 2)
                    dve.tensor_copy(par[:, CONV:PARAMS], ps[:, 2, 0:PARAMS - CONV]).then_inc(par_ready, 1)
                if g == 4:
                    dve.wait_ge(std_ready, 1)
                    dve.reciprocal(rs1, std1).then_inc(stat_ready, 1)
                    dve.wait_ge(stat_ready, 1)
                    diagonal(diag1, rs1)
                c = (g - 5) // 4
                if (g - 5) % 4 == 0 and 0 <= c < 5:
                    dve.wait_ge(granule_used, g - 1)
                    b = 2 * (c % 2)
                    dst = gproj[:, :, 512 * c:512 * c + 512] if c < 3 else \
                        nav[:, :, 512 * (c - 3):512 * (c - 3) + 512]
                    for t in range(T):
                        ins = dve.tensor_scalar(dst[:, t, :], ps[:, b + t, :], rs1[:, t:t + 1], None,
                                                ALU.mult)
                    ins.then_inc(banks_free, 1)
                c = (g - G_NAQK - 3) // 2
                if (g - G_NAQK - 3) % 2 == 0 and 0 <= c < 8:
                    dve.wait_ge(cross_copied, c + 1)
                    b = 2 * ((5 + c) % 2)
                    qk = naqkT[:, 2 * c:2 * c + 2, :]
                    dve.tensor_tensor(qk, ps[:, b:b + 2, 0:S], cross[:, :, :], ALU.add)\
                        .then_inc(banks_free, 1)
                    dve.wait_ge(banks_free, 6 + c)
                    dve.wait_ge(rms_ready, 1)
                    dve.tensor_tensor(qk, qk, over_heads(rms1[:, :], 2), ALU.mult).then_inc(qk_summed, 1)
                for i, (step, t) in enumerate(((0, 0), (0, 1), (1, 0), (2, 0), (1, 1), (2, 1))):
                    if g == 14 + i:
                        if i == 0:
                            dve.wait_ge(banks_free, 3)
                        rope(step, t)
                a = g - A_SCORES - 2
                if 0 <= a < HEADS:
                    dve.wait_ge(scored, a + 1)
                    if a < GH:
                        dve.tensor_reduce(smax[:, a, :], scores_ps, AX.X, ALU.max).then_inc(max_ready, 1)
                        dve.wait_ge(max_ready, a + 1)
                        dve.tensor_scalar(nmax[:, a, :], smax[:, a, :], -SCALE, None, ALU.mult)\
                            .then_inc(nmax_ready, 1)
                    else:
                        n = a - GH
                        if n == 0:
                            dve.wait_ge(bias_masked, 4)
                        for t in range(T):
                            j0 = 2 - 2 * t
                            rev = bass.AP(bias, (n * 6 + j0) * GW + GW - 1,
                                          [[NAH * 6 * GW, P], [GW, ROWS], [-1, GW]])
                            dve.scalar_tensor_tensor(
                                out=biased[:, t, :].rearrange("p (r m) -> p r m", r=ROWS),
                                in0=scores_ps[:, t, :].rearrange("p (r m) -> p r m", r=ROWS),
                                scalar=SCALE, in1=rev, op0=ALU.mult, op1=ALU.add).then_inc(biased_ready, 1)
                        dve.wait_ge(biased_ready, 2 * n + 2)
                        dve.tensor_reduce(nmax[:, a, :], biased[:, :, :], AX.X, ALU.max, negate=True)\
                            .then_inc(nmax_ready, 1)
                    dve.wait_ge(exp_done, 2 * a + 2)
                    dve.reciprocal(rsum[:, a, :], esum[:, a, :]).then_inc(rsum_ready, 1)
                    dve.wait_ge(rsum_ready, a + 1)
                    for t in range(T):
                        dve.tensor_scalar(prob[:, a % 2, t, :], prob[:, a % 2, t, :], rsum[:, a, t:t + 1],
                                          None, ALU.mult).then_inc(prob_ready, 1)
                a = g - A_PV - 2
                if 0 <= a < HEADS:
                    dve.wait_ge(o_hi, a + 1)
                    tile = (a + NAH) % KT
                    dve.scalar_tensor_tensor(out=oT[:, tile, S:2 * S],
                                             in0=ps[:, 6, 0:S],
                                             scalar=par[:, NAG + tile:NAG + tile + 1],
                                             in1=oT[:, tile, 0:S].bitcast(F32), op0=ALU.mult,
                                             op1=ALU.subtract).then_inc(o_lo, 1)
                for i, last in ((0, GH), (1, HEADS)):
                    if g == A_SUMSQ + last - 1 + 2:
                        dve.wait_ge(head_summed, last)
                        dve.tensor_reduce(ssqo[:, i, :],
                                          headsq_ps[:, last - 8:last, :].rearrange("p a t -> p t a"),
                                          AX.X, ALU.add).then_inc(osum_ready, 1)
                        dve.wait_ge(ostd_ready, i + 1)
                        dve.reciprocal(rso[:, i, :], stdo[:, i, :]).then_inc(ors_ready, 1)
                c = (g - G_OUT - 3) // 2
                if (g - G_OUT - 3) % 2 == 0 and 0 <= c < 8:
                    dve.wait_ge(granule_used, g - 1)
                    dve.wait_ge(ors_ready, c // 4 + 1)
                    b = 2 * ((C_OUT + c) % 2)
                    cs = slice(512 * (c % 4), 512 * (c % 4) + 512)
                    if c >= 4:
                        dve.wait_ge(banks_free, C_OUT + c - 3)
                    for t in range(T):
                        ins = dve.scalar_tensor_tensor(out=res[:, t, cs], in0=ps[:, b + t, :],
                                                       scalar=rso[:, c // 4, t:t + 1], in1=res[:, t, cs],
                                                       op0=ALU.mult, op1=ALU.add)
                    ins.then_inc(banks_free, 1)
                    if c >= 4:
                        turned_lo(h2T, LN2, KT, range(4 * (c - 4), 4 * (c - 3)))
                if g == 46:
                    for e in (0, S + 1):
                        dve.memset(u[:, :, :, e:e + 1], 0.0).then_inc(pads_zero, 1)
            dve.wait_ge(squared, T + 8)
            dve.tensor_reduce(ssq2, ssq2p, AX.X, ALU.add).then_inc(stat_ready, 1)
            dve.wait_ge(std_ready, 2)
            dve.reciprocal(rs2, std2).then_inc(stat_ready, 1)
            dve.wait_ge(stat_ready, 3)
            diagonal(diag2, rs2)
            split_at(G_UP + 2)
            dve.wait_ge(pads_zero, 2)
            dve.wait_ge(rms_ready, 2)

            def act_low(c):
                dve.wait_ge(act_hi, c + 1)
                tiles = bass.ds(c * 2, 2)
                dve.tensor_tensor(actT[:, tiles, S:2 * S], prod[:, :, :],
                                  actT[:, tiles, 0:S].bitcast(F32), ALU.subtract).then_inc(act_lo, 1)

            def up_chunk(c, first):
                for j in range(4):
                    g = G_UP + 3 + j
                    split_lo(g % RAW, g % HIS, c * 4 + (g + 1))
                    half = j // 2
                    if j % 2 == 0:
                        b = 2 * ((C_UP + half) % 2)
                        dve.wait_ge(cross_copied, c * 2 + (8 + half + 1))
                        uc = u[:, half, :, 1:S + 1]
                        dve.tensor_tensor(uc, ps[:, b:b + 2, 0:S], cross[:, :, :], ALU.add)\
                            .then_inc(banks_free, 1)
                        dve.wait_ge(banks_free, c * 2 + (C_UP + half + 1))
                        dve.tensor_tensor(uc, uc, over_heads(rms2[:, :], 2), ALU.mult).then_inc(u_ready, 1)
                        if half == 0 and not first:
                            act_low(c - 1)
                        continue
                    dve.wait_ge(centre_ready, c * 4 + (2 * half + 2))
                    for f in range(2):
                        col = c * 2 + (CONV + half * FT + f)
                        dve.scalar_tensor_tensor(out=y[:, half, f, :], in0=u[:, half, f, 0:S],
                                                 scalar=par[:, bass.ds(col, 1)], in1=y[:, half, f, :],
                                                 op0=ALU.mult, op1=ALU.add).then_inc(tap_done, 1)
                    for f in range(2):
                        dve.wait_ge(tap_done, c * 4 + (2 * half + f + 1))
                        col = c * 2 + (CONV + 4 * FT + half * FT + f)
                        dve.scalar_tensor_tensor(out=y[:, half, f, :], in0=u[:, half, f, 2:S + 2],
                                                 scalar=par[:, bass.ds(col, 1)], in1=y[:, half, f, :],
                                                 op0=ALU.mult, op1=ALU.add).then_inc(conv_ready, 1)
                    if half == 1:
                        dve.wait_ge(silu_ready, c + 1)
                        dve.wait_ge(conv_ready, c * 4 + 4)
                        dve.tensor_tensor(prod[:, :, :], y[:, 0], y[:, 1], ALU.mult).then_inc(prod_ready, 1)

            up_chunk(0, True)
            with dve.Fori(1, UPC) as c:
                up_chunk(c, False)
            act_low(UPC - 1)
            split_at(G_DOWN + 3)
            with dve.Fori(0, DROW) as b:
                for j in range(4):
                    g = G_DOWN + 4 + j
                    split_lo(g % RAW, g % HIS, b * 4 + (g + 1))

            def add_ffn(cb, used):
                dve.wait_ge(granule_used, used)
                cs = slice(512 * cb, 512 * cb + 512)
                for t in range(T):
                    dve.tensor_tensor(res[:, t, cs], ps[:, (4 + 2 * cb + t) % 8, :], res[:, t, cs], ALU.add)\
                        .then_inc(x2_ready, 1)
                dve.wait_ge(fgain_loaded, 16)
                for t in range(T):
                    dve.wait_ge(x2_ready, 2 * cb + t + 1)
                    dve.tensor_tensor(yout[:, t, cs], res[:, t, cs], fgain[:, cs], ALU.mult)\
                        .then_inc(gained, 1)

            for n in range(4 * DROW + 4, 4 * DNB):
                split_at(G_DOWN + n)
                if (n - 4 * DROW - 4) % 3 == 0:
                    add_ffn((n - 4 * DROW - 4) // 3, G_DOWN + n - 1)
            add_ffn(3, G_END)
            dve.wait_ge(squared, T + 8 + 8)
            dve.tensor_reduce(ssq3, ssq3p, AX.X, ALU.add).then_inc(stat_ready, 1)
            dve.wait_ge(std_ready, 3)
            dve.reciprocal(rs3, std3).then_inc(stat_ready, 1)
            dve.wait_ge(stat_ready, 5)
            dve.wait_ge(gained, 8)
            for h in range(2):
                cs = slice(h * D // 2, (h + 1) * D // 2)
                dve.tensor_scalar(yout[:, 0, cs], yout[:, 0, cs], rs3[:, 0:1], None, ALU.mult)\
                    .then_inc(y_ready[0], 1)

        @block.tensor
        def _(pe):
            def turn_tiles(n0, tiles):
                for k in tiles:
                    if k >= 8 and k % 2 == 0:
                        pe.wait_ge(tile_lo, n0 + k - 6)
                    b, h = 4 + (k // 2) % 4, k % 2
                    for t in range(T):
                        mm = pe.transpose(ps[:, b, S * h + P * t:S * h + P * t + P],
                                          res[:, t, P * k:P * k + P], ident[:, :])
                    mm.then_inc(tile_turned, 1)

            def spread(diag, n):
                pe.wait_ge(diag_ready, n)
                mm = pe.matmul(ps[:, 7, 0:S], ones[:, :], diag[:, :, :], start=True, stop=True)
                mm.then_inc(rms_spread, 1)

            def turn_column(cb):
                pe.wait_ge(banks_free, C_OUT + 4 + cb + 1)
                if cb == 0:
                    pe.wait_ge(ors_ready, 2)
                turn_tiles(KT, range(4 * cb, 4 * cb + 4))

            def tokens_granule(tok, k0, banks, raw_slot, hi_slot, first, last):
                hi = whi[:, hi_slot, :].rearrange("p (k n) -> p k n", k=4)
                lo = wlo[:, raw_slot, :].rearrange("p (k n) -> p k n", k=4)
                for kk in range(4):
                    k = k0 + kk
                    for t, b in enumerate(banks):
                        o = ps[:, b, :]
                        th, tl = tok[:, k, P * t:P * t + P], tok[:, k, S + P * t:S + P * t + P]
                        pe.matmul(o, th, hi[:, kk, :], start=first and kk == 0, stop=False)
                        pe.matmul(o, th, lo[:, kk, :], start=False, stop=False)
                        mm = pe.matmul(o, tl, hi[:, kk, :], start=False, stop=last and kk == 3)
                mm.then_inc(granule_used, 1)

            def weights_granule(tok, k0, banks, raw_slot, hi_slot):
                hi = whi[:, hi_slot, :].rearrange("p (k n) -> p k n", k=8)
                lo = wlo[:, raw_slot, :].rearrange("p (k n) -> p k n", k=8)
                for f, b in enumerate(banks):
                    for kk in range(8):
                        k = k0 + kk
                        pe.matmul(ps[:, b, :], hi[:, kk, P * f:P * f + P], tok[:, k, :],
                                  start=k == 0, stop=False, skip_group_check=True)
                        mm = pe.matmul(ps[:, b, S:2 * S], lo[:, kk, P * f:P * f + P], tok[:, k, 0:S],
                                       start=False, stop=k == KT - 1, skip_group_check=True)
                mm.then_inc(granule_used, 1)

            pe.wait_ge(ident_ready, 1)
            pe.wait_ge(gains_loaded, 16 * 4)
            pe.transpose(ps[:, 0, 0:CONV], stage[0:CONV, 0, :], ident[0:CONV, 0:CONV])\
                .then_inc(par_in_psum, 1)
            for h in range(2):
                pe.wait_ge(x_loaded[h], 16)
                turn_tiles(0, range(8 * h, 8 * h + 8))

            for g in range(G_UP):
                pe.wait_ge(lo_ready, g + 1)
                if g < G_NAQK:
                    chunk, kq = divmod(g, 4)
                    if chunk == 0:
                        pe.wait_ge(tile_lo, 4 * kq + 4)
                    if kq == 0 and chunk == 1:
                        pe.wait_ge(par_ready, 2)
                    if kq == 0 and chunk >= 2:
                        pe.wait_ge(banks_free, chunk - 1)
                    b = 2 * (chunk % 2)
                    tokens_granule(xT, 4 * kq, (b, b + 1), g % RAW, g % HIS, kq == 0, kq == 3)
                elif g < G_OUT:
                    c, kh = divmod(g - G_NAQK, 2)
                    chunk = 5 + c
                    if kh == 0:
                        pe.wait_ge(banks_free, chunk - 1)
                    b = 2 * (chunk % 2)
                    weights_granule(xT, 8 * kh, (b, b + 1), g % RAW, g % HIS)
                else:
                    c, kh = divmod(g - G_OUT, 2)
                    chunk = C_OUT + c
                    if kh == 0:
                        pe.wait_ge(banks_free, chunk - 1)
                    if c in (0, 4):
                        pe.wait_ge(o_lo, GH if c == 0 else HEADS)
                    b = 2 * (chunk % 2)
                    tokens_granule(oT, (NAH if c < 4 else 0) + 4 * kh, (b, b + 1), g % RAW, g % HIS,
                                   kh == 0, kh == 1)

                if g == 0:
                    pe.wait_ge(conv_loaded, 16 * 4)
                    for j in range(4):
                        mm = pe.transpose(ps[:, 2, 2 * FT * j:2 * FT * (j + 1)], stage[0:2 * FT, 1 + j, :],
                                          ident[0:2 * FT, 0:2 * FT])
                    mm.then_inc(par_in_psum, 1)
                if g == 5:
                    pe.wait_ge(ones_ready, 1)
                    spread(diag1, 1)
                if 20 <= g < 25:
                    i = g - 20
                    if i == 0:
                        pe.wait_ge(rope_step, 21)
                    else:
                        pe.wait_ge(g_copied, i)
                    h0 = (2 * (i - 1)) % 10
                    for h in range(2):
                        for t in range(T):
                            mm = pe.transpose(ps[:, 7, S * h + P * t:S * h + P * t + P],
                                              gproj[:, t, DH * (h0 + h):DH * (h0 + h) + DH], ident[:, :])
                    mm.then_inc(g_turned, 1)
                a = g - A_SCORES
                if 0 <= a < HEADS:
                    if a < GH:
                        pe.wait_ge(g_copied, 2 + a // 2)
                        q, k = gT[:, a, :], gT[:, GH + a // (GH // GKV), :]
                    else:
                        n = a - GH
                        pe.wait_ge(qk_summed, 2 + 2 * (n // 2))
                        i = 4 * (n // 2) + n % 2
                        q, k = naqkT[:, i, :], naqkT[:, i + 2, :]
                    if a >= 1:
                        pe.wait_ge(exp_done, 2 * a)
                    for t in range(T):
                        mm = pe.matmul(scores_ps[:, t, :], q[:, P * t:P * t + P], k, start=True, stop=True)
                    mm.then_inc(scored, 1)
                a = g - A_TRANSPOSE
                if 0 <= a < HEADS:
                    pe.wait_ge(prob_ready, 2 * a + 2)
                    if a >= 1:
                        pe.wait_ge(probT_ready, a)
                    for k in range(T):
                        for t in range(T):
                            mm = pe.transpose(probT_ps[:, k, P * t:P * t + P],
                                              prob[:, a % 2, t, P * k:P * k + P], ident[:, :])
                    mm.then_inc(prob_turned, 1)
                a = g - A_PV
                if 0 <= a < HEADS:
                    pe.wait_ge(probT_ready, a + 1)
                    if a >= 1:
                        pe.wait_ge(o_lo, a)
                    for k in range(T):
                        if a < GH:
                            v0 = (GH + GKV + a // (GH // GKV)) * DH
                            v = gproj[:, k, v0:v0 + DH]
                        else:
                            v = nav[:, k, DH * (a - GH):DH * (a - GH) + DH]
                        mm = pe.matmul(ps[:, 6, 0:S], v, probT[:, a % 2, k, :],
                                       start=k == 0, stop=k == T - 1)
                    mm.then_inc(pv_done, 1)
                a = g - A_SUMSQ
                if 0 <= a < HEADS:
                    pe.wait_ge(osq_ready, a + 1)
                    if a == 0:
                        pe.wait_ge(g_copied, 5)
                    if a == GH:
                        pe.wait_ge(osum_ready, 1)
                    for t in range(T):
                        mm = pe.matmul(headsq_ps[:, a, t:t + 1], osq[:, P * t:P * t + P], ones[:, 0:1],
                                       start=True, stop=True)
                    mm.then_inc(head_summed, 1)
                c = (g - G_OUT - 10) / 2
                if c in (0, 1, 2):
                    turn_column(int(c))

            def up_granule(c, j):
                g = G_UP + j
                pe.wait_ge(lo_ready, c * 4 + (g + 1))
                chunk = C_UP + j // 2
                if j % 2 == 0:
                    pe.wait_ge(banks_free, c * 2 + (chunk - 1))
                b = 2 * (chunk % 2)
                weights_granule(h2T, 8 * (j % 2), (b, b + 1), g % RAW, g % HIS)

            pe.wait_ge(tile_lo, KT + 8)
            up_granule(0, 0)
            turn_column(3)
            pe.wait_ge(tile_lo, 2 * KT)
            up_granule(0, 1)
            spread(diag2, 2)
            up_granule(0, 2)
            up_granule(0, 3)
            with pe.Fori(1, UPC) as c:
                for j in range(4):
                    up_granule(c, j)

            for n, (blk, cb) in enumerate(DOWN):
                g = G_DOWN + n
                pe.wait_ge(lo_ready, g + 1)
                if cb == 0:
                    pe.wait_ge(act_lo, 2 * blk + 2)
                if n == 2:
                    pe.wait_ge(banks_free, C_UP + 2 * UPC)
                b = (4 + 2 * cb) % 8
                tokens_granule(actT, 4 * blk, (b, b + 1), g % RAW, g % HIS, blk == 0, blk == DNB - 1)


_INS = ["x", "ln1_g", "w_in", "na_rpb", "q_norm_g", "k_norm_g", "na_out_g", "gqa_out_g", "w_out",
        "ln2_g", "w_up", "conv_w", "conv_b", "w_down", "final_g"]


def kernel(**inputs):
    import numpy as _np
    import concourse.bacc as _bacc
    from concourse import mybir as _mybir
    from concourse.bass_utils import run_bass_kernel_spmd as _run

    nc = _bacc.Bacc("TRN2", target_bir_lowering=False, num_devices=1)
    arrays, args = {}, []

    def give(name, a):
        arrays[f"in_{name}_dram"] = a
        args.append(nc.dram_tensor(f"in_{name}_dram", a.shape, _mybir.dt.from_np(a.dtype),
                                   kind="ExternalInput").ap())

    for name in _INS:
        a = _np.asarray(inputs[name])
        if name == "na_rpb":
            a = a[..., ::-1]
        give(name, _np.ascontiguousarray(a))
    t = _np.arange(S)
    inv = (1.0 / (10000.0 ** (_np.arange(0, DH // 2, 2, dtype=_np.float32) / (DH // 2)))).astype(_np.float32)
    ang = _np.concatenate([(t // GW).astype(_np.float32)[:, None] * inv,
                           (t % GW).astype(_np.float32)[:, None] * inv], axis=-1)
    give("cos", _np.repeat(_np.cos(ang), 2, axis=-1).astype(_np.float32))
    give("sin", _np.stack([-_np.sin(ang), _np.sin(ang)], axis=-1).reshape(S, DH).astype(_np.float32))
    args.append(nc.dram_tensor("out_0_dram", (1, S, D), F32, kind="ExternalOutput").ap())
    hybrid_block(nc, *args)
    r = _run(nc, [arrays], core_ids=[0])
    return r.results[0]["out_0_dram"]
```

```python
from contextlib import ExitStack

import concourse.bass as bass
from concourse import mybir
from concourse.alu_op_type import AluOpType as ALU

ACT = mybir.ActivationFunctionType
AX = mybir.AxisListType
F32 = mybir.dt.float32
F32R = mybir.dt.float32r

P = 128
D = 2048
S = 256
T = S // P
KT = D // P
DH = 128
NAH = 8
GH = 8
GKV = 2
GW = 64
ROWS = S // GW
RPB_R, RPB_C = 15, 31
FF = 5632
FT = FF // P
EPS = 1e-6
SCALE = float(DH) ** -0.5
MASKED = -1.0e30

RAW = 4
HIS = 2
PIECES = (4, 4, 2, 2)
G_GQA = 0
G_NAV = G_GQA + 12
G_NAQK = G_NAV + 8
G_OUT = G_NAQK + 16
G_UP = G_OUT + 16
UPC = FF // 256
G_DOWN = G_UP + 4 * UPC
DNB = FT // 4
DROW = 8
G_END = G_DOWN + 4 * DNB

WARM1, WARM2 = 3, 3

C_OUT = 13
C_UP = C_OUT + 8

A_TURN = 21
A_SCORES = 24
A_TRANSPOSE = A_SCORES + 2
A_PV = A_SCORES + 3
A_SUMSQ = A_SCORES + 4
HEADS = GH + NAH

NAQK_SPLIT = (30, 33, 35, 38)

DOWN = [(b, cb) for b in range(DROW) for cb in range(4)] + \
       [(b, cb) for cb in range(4) for b in range(DROW, DNB)]

LN1, LN2, NAG, GQAG = 0, KT, 2 * KT, 2 * KT + NAH
CONV = 2 * KT + NAH + GH
PARAMS = CONV + 4 * 2 * FT


def hybrid_block(nc, x, w_in, na_rpb, q_norm_g, k_norm_g, w_out, w_up, w_down, final_g, gains, conv,
                 cos_t, sin_t, out):
    with ExitStack() as ctx:
        sem = lambda name: ctx.enter_context(nc.semaphore(name))

        BASE = 16512
        A_RES = BASE
        A_X = A_RES + T * D * 4
        A_E = A_X + KT * 2 * S * 4
        A_O = A_E + 57344
        A_RAW = A_O + KT * 2 * S * 4
        A_HI = A_RAW + RAW * 8192
        A_M = A_HI + HIS * 8192

        def at(name, shape, dt, offset):
            return nc.alloc_sbuf_tensor_at(name, shape, dt, offset=offset)

        res = at("res", [P, T, D], F32, A_RES)
        xT = at("xT", [P, KT, 2 * S], F32R, A_X)
        naqkT = at("naqkT", [P, 2 * NAH, S], F32, A_E)
        nav = at("nav", [P, T, NAH * DH], F32, A_E + 16384)
        gproj = at("gproj", [P, T, 1536], F32, A_E + 24576)
        gT_hi = at("gT_hi", [P, GH + GKV, S], F32R, A_E + 36864)
        gT_lo = at("gT_lo", [P, GH + GKV, S], F32R, A_O + 6144)
        naqk_lo = at("naqk_lo", [P, 2 * NAH, S], F32R, A_E)
        naqk_hi = [at("naqk_hi0", [P, 4, S], F32R, A_O + 28672),
                   at("naqk_hi1", [P, 4, S], F32R, A_O + 6144),
                   at("naqk_hi2", [P, 4, S], F32R, A_O + 10240),
                   at("naqk_hi3", [P, 4, S], F32R, A_E + 36864 + 4096)]
        prob = at("prob", [P, 2, T, S], F32, A_E + 47104)
        probT_hi = at("probT_hi", [P, 2, T, S], F32R, A_E + 51200)
        probT_lo = [at("probT_lo_gqa", [P, 2, T, S], F32R, A_O + 2048),
                    at("probT_lo_na", [P, 2, T, S], F32R, A_E + 36864)]
        gv_hi = at("gv_hi", [P, T, GKV * DH], F32R, A_O)
        gproj_r = at("gproj_r", [P, T, 1536], F32R, A_E + 24576)
        nav_lo = at("nav_lo", [P, T, NAH * DH], F32R, A_E + 16384)
        GV = (GH + GKV) * DH
        osq = at("osq", [P, S], F32, A_E + 55296)
        rms1 = at("rms1", [P, S], F32, A_E + 56320)
        oT = at("oT", [P, KT, 2 * S], F32R, A_O)
        h2T = at("h2T", [P, KT, 2 * S], F32R, A_X)
        junk1 = at("junk1", [P, T, D], F32, A_O)
        junk2 = at("junk2", [P, T, D], F32, A_E)
        stage = at("stage", [P, 5, P], F32, A_O + 16384)
        head_junk = at("head_junk", [P, T, 10, DH], F32, A_O + 16384)
        rot_n = at("rot_n", [P, 10, DH], F32, A_O + 16384)
        rot_m = at("rot_m", [P, 10, DH], F32, A_O + 16384 + 5120)
        diag1 = at("diag1", [P, T, P], F32, A_O + 29696)
        cosr = at("cosr", [P, T, DH], F32, A_O + 26624)
        sinr = at("sinr", [P, T, DH], F32, A_O + 27648)
        grow = at("grow", [P, 2, DH], F32, A_O + 28672)
        actT = at("actT", [P, FT, 2 * S], F32R, A_E)
        fgain = at("fgain", [P, D], F32, A_X)
        yout = at("yout", [P, T, D], F32, A_X + 8192)
        junk3 = at("junk3", [P, T, 512], F32, A_X + 24576)
        raw = at("raw", [P, RAW, 2048], F32, A_RAW)
        wlo = at("wlo", [P, RAW, 2048], F32R, A_RAW)
        whi = at("whi", [P, HIS, 2048], F32R, A_HI)
        par = at("par", [P, PARAMS], F32, A_M)
        stat = at("stat", [P, 256], F32, A_M + 1600)
        ident = at("ident", [P, P], F32, A_M + 2624)
        eps = at("eps", [P, 1], F32, A_M + 3136)
        ones = at("ones", [P, P], F32, A_M + 3168)
        A_W = A_M + 3680
        bias = at("bias", [P, NAH, 6, GW], F32, A_W)
        u = at("u", [P, 2, 2, S + 2], F32, A_W)
        y = at("y", [P, 2, 2, S], F32, A_W + 4160)
        prod = at("prod", [P, 2, S], F32, A_W + 8256)
        rms2 = at("rms2", [P, S], F32, A_W + 10304)
        diag2 = at("diag2", [P, T, P], F32, A_W + 16384)
        cosg = at("cosg", [P, T, 2, DH], F32, A_W + 12288)
        sing = at("sing", [P, T, 2, DH], F32, A_W + 14336)
        osum = at("osum", [P, 2, S], F32, A_W + 12288)
        biased = at("biased", [P, T, S], F32, A_W + 16384)
        cross = at("cross", [P, 2, S], F32, A_W + 18432)

        ps = ctx.enter_context(nc.psum_tensor("ps", [P, 8, 512], F32))
        scores_ps = ps[:, 4, :].rearrange("p (t k) -> p t k", t=T)
        probT_ps = ps[:, 5, :].rearrange("p (k q) -> p k q", k=T)

        ssq1, std1, rs1 = stat[:, 0:2], stat[:, 2:4], stat[:, 4:6]
        ssq2p = stat[:, 8:16].rearrange("p (t c) -> p t c", t=T)
        ssq2, std2, rs2 = stat[:, 16:18], stat[:, 18:20], stat[:, 20:22]
        ssq3, std3, rs3 = stat[:, 24:26], stat[:, 26:28], stat[:, 28:30]
        ssq3p = stat[:, 240:248].rearrange("p (t c) -> p t c", t=T)
        ssqg = stat[:, 32:52].rearrange("p (t h) -> p t h", t=T)
        stdg = stat[:, 52:72].rearrange("p (t h) -> p t h", t=T)
        rsg = stat[:, 72:92].rearrange("p (t h) -> p t h", t=T)
        stdo = stat[:, 100:104].rearrange("p (g t) -> p g t", g=2)
        rso = stat[:, 104:108].rearrange("p (g t) -> p g t", g=2)
        smax = stat[:, 112:144].rearrange("p (a t) -> p a t", t=T)
        nmax = stat[:, 144:176].rearrange("p (a t) -> p a t", t=T)
        esum = stat[:, 176:208].rearrange("p (a t) -> p a t", t=T)
        rsum = stat[:, 208:240].rearrange("p (a t) -> p a t", t=T)
        turned_heads = ps[:, 7, :].rearrange("p (h s) -> p h s", h=2)
        headsq_ps = ps[:, 7, 0:4].rearrange("p (g t) -> p g t", t=T)

        x_loaded = [sem(f"x_loaded{h}") for h in range(4)]
        gains_loaded, conv_loaded = sem("gains_loaded"), sem("conv_loaded")
        rope_loaded = sem("rope_loaded")
        bias_loaded = sem("bias_loaded")
        fgain_loaded = sem("fgain_loaded")
        stored = sem("stored")
        w_loaded = [sem(f"w_loaded{i}") for i in range(RAW)]
        piece_loaded = [[sem(f"piece_loaded{g}_{i}") for i in range(n - 1)] for g, n in enumerate(PIECES)]
        piece_hi, piece_lo = sem("piece_hi"), sem("piece_lo")
        hi_ready = sem("hi_ready")
        lo_ready = sem("lo_ready")
        granule_used = sem("granule_used")
        banks_free = sem("banks_free")
        ident_zero, ident_ready = sem("ident_zero"), sem("ident_ready")
        ones_ready, eps_ready = sem("ones_ready"), sem("eps_ready")
        bias_masked = sem("bias_masked")
        par_in_psum, par_ready = sem("par_in_psum"), sem("par_ready")
        squared, std_ready, stat_ready = sem("squared"), sem("std_ready"), sem("stat_ready")
        diag_ready, rms_spread, rms_ready = sem("diag_ready"), sem("rms_spread"), sem("rms_ready")
        tile_turned = sem("tile_turned")
        tile_hi, tile_lo = sem("tile_hi"), sem("tile_lo")
        cross_copied = sem("cross_copied")
        tables_ready = sem("tables_ready")
        rope_step = sem("rope_step")
        head_squared = sem("head_squared")
        stdg_ready = sem("stdg_ready")
        g_turned, g_hi, g_lo = sem("g_turned"), sem("g_hi"), sem("g_lo")
        qk_hi, qk_lo = sem("qk_hi"), sem("qk_lo")
        scored = sem("scored")
        biased_ready = sem("biased_ready")
        max_ready, nmax_ready = sem("max_ready"), sem("nmax_ready")
        exp_done = sem("exp_done")
        rsum_ready, prob_ready = sem("rsum_ready"), sem("prob_ready")
        prob_turned = sem("prob_turned")
        probT_hi_ready, probT_lo_ready = sem("probT_hi_ready"), sem("probT_lo_ready")
        v_hi_ready, v_lo_ready = sem("v_hi_ready"), sem("v_lo_ready")
        pv_done = sem("pv_done")
        osq_ready, o_hi, o_lo = sem("osq_ready"), sem("o_hi"), sem("o_lo")
        osum_zero, osq_summed = sem("osum_zero"), sem("osq_summed")
        group_summed, ostd_ready, ors_ready = sem("group_summed"), sem("ostd_ready"), sem("ors_ready")
        pads_zero = sem("pads_zero")
        u_ready, centre_ready = sem("u_ready"), sem("centre_ready")
        qk_summed = sem("qk_summed")
        tap_done, conv_ready = sem("tap_done"), sem("conv_ready")
        silu_ready, prod_ready = sem("silu_ready"), sem("prod_ready")
        act_hi, act_lo = sem("act_hi"), sem("act_lo")
        down_tile0 = sem("down_tile0")
        x2_ready, gained = sem("x2_ready"), sem("gained")
        y_ready = [sem(f"y_ready{h}") for h in range(2)]

        w_in_v = w_in[0].rearrange("(k p) n -> p k n", p=P)
        w_out_v = w_out[0].rearrange("(k p) n -> p k n", p=P)
        w_up_v = w_up[0].rearrange("(k p) n -> p k n", p=P)
        w_down_v = w_down[0].rearrange("(b k p) n -> b p k n", p=P, k=4)
        NA_W = NAH * DH

        def source(g):
            if g < G_NAQK:
                c, kq = divmod(g, 4)
                col = 3 * NA_W + 512 * c if c < 3 else 2 * NA_W + 512 * (c - 3)
                return w_in_v[:, 4 * kq:4 * kq + 4, col:col + 512]
            if g < G_OUT:
                c, kh = divmod(g - G_NAQK, 2)
                col = (c % 2) * NA_W + 256 * (c // 2)
                return w_in_v[:, 8 * kh:8 * kh + 8, col:col + 256]
            c, kh = divmod(g - G_OUT, 2)
            k = (NAH if c < 4 else 0) + 4 * kh
            return w_out_v[:, k:k + 4, 512 * (c % 4):512 * (c % 4) + 512]

        def piece(g, i):
            w = 2048 // PIECES[g]
            return slice(w * i, w * i + w)

        def pieces_before(g, i):
            return sum(n - 1 for n in PIECES[:g]) + i + 1

        block = ctx.enter_context(nc.Block())

        @block.sync
        def _(sp):
            xv = x[0].rearrange("(t p) d -> p t d", p=P)
            sp.dma_start(stage[0:CONV, 0, :], gains).then_inc(gains_loaded, 16)

            def load_x(h):
                cs = slice(h * D // 4, (h + 1) * D // 4)
                sp.dma_start(res[:, :, cs], xv[:, :, cs]).then_inc(x_loaded[h], 16)

            load_x(0)

            def load(slot, src):
                k = src.shape[1]
                dst = raw[:, slot, :].rearrange("p (k n) -> p k n", k=k)
                sp.dma_start(dst, src).then_inc(w_loaded[slot], 16)

            for g, n in enumerate(PIECES):
                for i in range(n):
                    tiles = slice(4 // n * i, 4 // n * (i + 1))
                    dst = raw[:, g, piece(g, i)].rearrange("p (k n) -> p k n", k=4 // n)
                    sp.dma_start(dst, source(g)[:, tiles, :])\
                        .then_inc(w_loaded[g] if i == n - 1 else piece_loaded[g][i], 16)
                    if g < 3 and i == n // 2 - 1:
                        load_x(g + 1)
            for g in range(len(PIECES), G_UP):
                sp.wait_ge(granule_used, g - RAW + 1)
                load(g % RAW, source(g))
            with sp.Fori(0, UPC) as c:
                for j in range(4):
                    sp.wait_ge(granule_used, c * 4 + (G_UP + j - RAW + 1))
                    col = c * 256 + (j // 2) * FF
                    load((G_UP + j) % RAW, w_up_v[:, 8 * (j % 2):8 * (j % 2) + 8, bass.ds(col, 256)])
            with sp.Fori(0, DROW) as b:
                for j in range(4):
                    sp.wait_ge(granule_used, b * 4 + (G_DOWN + j - RAW + 1))
                    src = w_down_v[bass.ds(b, 1), :, :, 512 * j:512 * j + 512].rearrange(
                        "o p k n -> (o p) k n")
                    load((G_DOWN + j) % RAW, src)
            sp.dma_start(fgain[:, :], final_g.rearrange("(o d) -> o d", o=1).broadcast_to([P, D]))\
                .then_inc(fgain_loaded, 16)
            for n in range(4 * DROW, 4 * DNB):
                b, cb = DOWN[n]
                sp.wait_ge(granule_used, G_DOWN + n - RAW + 1)
                load((G_DOWN + n) % RAW, w_down_v[b, :, :, 512 * cb:512 * cb + 512])
            ov = out[0].rearrange("(t p) d -> p t d", p=P)
            for t in range(T):
                for q in (0, 2, 1, 3):
                    sp.wait_ge(y_ready[q // 2], 2 * t + q % 2 + 1)
                    cs = slice(512 * q, 512 * q + 512)
                    sp.dma_start(ov[:, t, cs], yout[:, t, cs]).then_inc(stored, 16)
            sp.wait_ge(stored, 16 * 4 * T)

        @block.gpsimd
        def _(pool):
            pool.memset(ones[:, :], 1.0).then_inc(ones_ready, 1)
            pool.memset(ident[:, :], 0.0).then_inc(ident_zero, 1)
            pool.wait_ge(ident_zero, 1)
            pool.affine_select(out=ident[:, :], in_=ident[:, :], compare_op=ALU.not_equal, fill=1.0,
                               base=0, pattern=[[-1, P]], channel_multiplier=1).then_inc(ident_ready, 1)
            pool.wait_ge(bias_loaded, 16 * 2 * NAH)
            n = 0
            for half in range(2):
                b = bias[GW * half:GW * half + GW].rearrange("p h j m -> p (h j) m")
                left, right = b[:, :, 16:64], b[:, :, 0:48]
                pool.affine_select(out=left, in_=left, compare_op=ALU.is_ge, fill=MASKED, base=55,
                                   pattern=[[0, 6 * NAH], [-1, 48]], channel_multiplier=-1)\
                    .then_inc(bias_masked, 1)
                n += 1
                pool.wait_ge(bias_masked, n)
                pool.affine_select(out=right, in_=right, compare_op=ALU.is_ge, fill=MASKED, base=-56,
                                   pattern=[[0, 6 * NAH], [1, 48]], channel_multiplier=1)\
                    .then_inc(bias_masked, 1)
                n += 1
                pool.wait_ge(bias_masked, n)

            pool.wait_ge(rope_step, 17)
            pool.memset(osum[:, :, :], 0.0).then_inc(osum_zero, 1)
            pool.wait_ge(osum_zero, 1)
            for a in range(HEADS):
                pool.wait_ge(osq_ready, a + 1)
                if a % GH:
                    pool.wait_ge(osq_summed, a)
                pool.tensor_tensor(osum[:, a // GH, :], osum[:, a // GH, :], osq[:, :], ALU.add)\
                    .then_inc(osq_summed, 1)

        @block.scalar
        def _(act):
            act.preload_act_table(ACT.Sqrt)

            def split_hi(slot_raw, slot_hi, loaded, used):
                act.wait_ge(w_loaded[slot_raw], loaded)
                if used is not None:
                    act.wait_ge(granule_used, used)
                act.activation(whi[:, slot_hi, :], raw[:, slot_raw, :], ACT.Copy).then_inc(hi_ready, 1)

            def split_at(g):
                split_hi(g % RAW, g % HIS, 16 * (g // RAW + 1), g - HIS + 1 if g >= HIS else None)

            def turned_hi(dst, gain0, n0, tiles):
                for k in tiles:
                    act.wait_ge(tile_turned, n0 + k + 2 - k % 2)
                    b, h = 4 + (k // 2) % 4, k % 2
                    act.activation(dst[:, k, 0:S], ps[:, b, S * h:S * h + S], ACT.Copy,
                                   scale=par[:, gain0 + k:gain0 + k + 1]).then_inc(tile_hi, 1)

            for g, n in enumerate(PIECES):
                for i in range(n):
                    last = i == n - 1
                    act.wait_ge(w_loaded[g] if last else piece_loaded[g][i], 16)
                    if i == 0 and g >= HIS:
                        act.wait_ge(granule_used, g - HIS + 1)
                    act.activation(whi[:, g % HIS, piece(g, i)], raw[:, g, piece(g, i)], ACT.Copy)\
                        .then_inc(hi_ready if last else piece_hi, 1)
                    if (g, i) == (0, 0):
                        act.wait_ge(par_ready, 1)
                        turned_hi(xT, LN1, 0, range(4))
                    if g < 3 and i == n // 2:
                        turned_hi(xT, LN1, 0, range(4 * g + 4, 4 * g + 8))

            act.dma_start(stage[0:2 * FT, 1:5, :], conv.rearrange("j (f p) -> f j p", p=P))\
                .then_inc(conv_loaded, 16)
            for i, vec in enumerate((q_norm_g, k_norm_g)):
                act.dma_start(grow[:, i, :], vec.broadcast_to([P, DH])).then_inc(rope_loaded, 16)
            act.dma_start(cosr[:, :, :], cos_t.rearrange("(t p) d -> p t d", p=P)).then_inc(rope_loaded, 16)
            act.dma_start(sinr[:, :, :], sin_t.rearrange("(t p) d -> p t d", p=P)).then_inc(rope_loaded, 16)

            def load_bias(half, h):
                off = h * RPB_R * RPB_C + (5 - half) * RPB_C + 15 - (GW - 1)
                src = bass.AP(na_rpb.tensor, off, [[1, GW], [RPB_C, 6], [1, GW]])
                act.dma_start(bias[GW * half:GW * half + GW, h], src).then_inc(bias_loaded, 16)

            for g in range(len(PIECES), G_UP + 2):
                if A_TURN + 2 <= g < A_TURN + 7:
                    i = g - A_TURN - 2
                    act.wait_ge(g_turned, i + 1)
                    h0 = (2 * (i - 1)) % 10
                    act.activation(gT_hi[:, h0:h0 + 2, :], turned_heads, ACT.Copy).then_inc(g_hi, 1)
                split_at(g)
                if g < 6:
                    t = g - 4
                    for h in range(4):
                        act.wait_ge(x_loaded[h], 16)
                    act.activation(junk1[:, t, :], res[:, t, :], ACT.Square, accum_out=ssq1[:, t:t + 1])\
                        .then_inc(squared, 1)
                if g == 5:
                    act.wait_ge(squared, T)
                    act.wait_ge(eps_ready, 1)
                    act.activation(std1, ssq1, ACT.Sqrt, bias=eps[:, :], scale=1.0 / D).then_inc(std_ready, 1)
                if g == 10:
                    act.wait_ge(rms_spread, 1)
                    act.activation(rms1[:, :], ps[:, 7, 0:S], ACT.Copy).then_inc(rms_ready, 1)
                c = (g - G_NAQK - 3) // 2
                if (g - G_NAQK - 3) % 2 == 0 and 0 <= c < 8:
                    act.wait_ge(granule_used, g - 1)
                    if c >= 1:
                        act.wait_ge(banks_free, 5 + c)
                    b = 2 * ((5 + c) % 2)
                    act.activation(cross[:, :, :], ps[:, b:b + 2, S:2 * S], ACT.Copy)\
                        .then_inc(cross_copied, 1)
                if g in (14, 15):
                    t = g - 14
                    act.wait_ge(banks_free, 3)
                    if t == 0:
                        act.wait_ge(par_in_psum, 2)
                    for h in range(10):
                        act.activation(head_junk[:, t, h, :], gproj[:, t, DH * h:DH * h + DH], ACT.Square,
                                       accum_out=ssqg[:, t, h:h + 1]).then_inc(head_squared, 1)
                if g == 16:
                    act.activation(gv_hi[:, :, :], gproj[:, :, GV:], ACT.Copy).then_inc(v_hi_ready, 1)
                if g in (28, 29):
                    t = g - 28
                    act.wait_ge(g_turned, 5)
                    act.wait_ge(banks_free, 5)
                    act.activation(gproj_r[:, t, 0:NAH * DH], nav[:, t, :], ACT.Copy)\
                        .then_inc(v_hi_ready, 1)
                if g == 15:
                    act.wait_ge(head_squared, 10 * T)
                    act.activation(stdg, ssqg, ACT.Sqrt, bias=eps[:, :], scale=1.0 / DH).then_inc(stdg_ready, 1)
                if 6 <= g < 6 + 2 * NAH:
                    load_bias((g - 6) // NAH, (g - 6) % NAH)
                if g in NAQK_SPLIT:
                    pair = NAQK_SPLIT.index(g)
                    act.wait_ge(qk_summed, 2 * pair + 2)
                    if pair >= 1:
                        act.wait_ge(scored, GH)
                    act.activation(naqk_hi[pair][:, :, :], naqkT[:, 4 * pair:4 * pair + 4, :], ACT.Copy)\
                        .then_inc(qk_hi, 1)
                a = g - A_PV - 2
                if 0 <= a < HEADS:
                    act.wait_ge(pv_done, a + 1)
                    if a >= 1:
                        act.wait_ge(osq_summed, a)
                    o = ps[:, 6, 0:S]
                    act.activation(osq[:, :], o, ACT.Square).then_inc(osq_ready, 1)
                    tile = (a + NAH) % KT
                    act.activation(oT[:, tile, 0:S], o, ACT.Copy, scale=par[:, NAG + tile:NAG + tile + 1])\
                        .then_inc(o_hi, 1)
                a = g - A_TRANSPOSE - 2
                if 0 <= a < HEADS:
                    act.wait_ge(prob_turned, a + 1)
                    if a >= 2:
                        act.wait_ge(pv_done, a - 1)
                    act.activation(probT_hi[:, a % 2], probT_ps, ACT.Copy).then_inc(probT_hi_ready, 1)
                a = g - A_SCORES - 2
                if 0 <= a < HEADS:
                    act.wait_ge(nmax_ready, a + 1)
                    if a >= 2:
                        act.wait_ge(prob_turned, a - 1)
                    for t in range(T):
                        src, sc = (scores_ps, SCALE) if a < GH else (biased, 1.0)
                        act.activation(prob[:, a % 2, t, :], src[:, t, :], ACT.Exp, bias=nmax[:, a, t:t + 1],
                                       scale=sc, accum_out=esum[:, a, t:t + 1]).then_inc(exp_done, 1)
                for i, last in ((0, GH), (1, HEADS)):
                    if g == A_SUMSQ + last - 1 + 2:
                        act.wait_ge(group_summed, i + 1)
                        act.activation(stdo[:, i, :], headsq_ps[:, i, :], ACT.Sqrt, bias=eps[:, :],
                                       scale=1.0 / (NAH * DH)).then_inc(ostd_ready, 1)
                c = (g - G_OUT - 3) // 2
                if (g - G_OUT - 3) % 2 == 0 and 4 <= c < 8:
                    act.wait_ge(banks_free, C_OUT + c + 1)
                    for t in range(T):
                        cs = slice(512 * (c - 4), 512 * (c - 4) + 512)
                        act.activation(junk2[:, t, cs], res[:, t, cs], ACT.Square,
                                       accum_out=ssq2p[:, t, c - 4:c - 3]).then_inc(squared, 1)
                c = (g - G_OUT - 4) // 2
                if (g - G_OUT - 4) % 2 == 0 and 4 <= c < 7:
                    turned_hi(h2T, LN2, KT, range(4 * (c - 4), 4 * (c - 3)))
            turned_hi(h2T, LN2, KT, range(12, 16))
            split_at(G_UP + 2)
            act.wait_ge(stat_ready, 2)
            act.activation(std2, ssq2, ACT.Sqrt, bias=eps[:, :], scale=1.0 / D).then_inc(std_ready, 1)
            act.preload_act_table(ACT.Silu)

            def act_high(c):
                act.wait_ge(prod_ready, c + 1)
                act.activation(actT[:, bass.ds(c * 2, 2), 0:S], prod[:, :, :], ACT.Copy).then_inc(act_hi, 1)

            def up_chunk(c, first):
                for j in range(4):
                    g = G_UP + 3 + j
                    split_hi(g % RAW, g % HIS, c * 16 + 16 * (g // RAW + 1), c * 4 + (g - HIS + 1))
                    half = j // 2
                    if first and j == 0:
                        act.wait_ge(rms_spread, 2)
                        act.activation(rms2[:, :], ps[:, 7, 0:S], ACT.Copy).then_inc(rms_ready, 1)
                    if j % 2 == 0:
                        b = 2 * ((C_UP + half) % 2)
                        act.wait_ge(granule_used, c * 4 + (G_UP + 2 * half + 2))
                        act.wait_ge(banks_free, c * 2 + (C_UP + half))
                        act.activation(cross[:, :, :], ps[:, b:b + 2, S:2 * S], ACT.Copy)\
                            .then_inc(cross_copied, 1)
                        if half == 0 and not first:
                            act_high(c - 1)
                        if half == 1:
                            act.wait_ge(conv_ready, c * 4 + 2)
                            act.activation(y[:, 0], y[:, 0], ACT.Silu).then_inc(silu_ready, 1)
                        continue
                    act.wait_ge(u_ready, c * 2 + (half + 1))
                    for f in range(2):
                        col = c * 2 + (CONV + 2 * FT + half * FT + f)
                        act.activation(y[:, half, f, :], u[:, half, f, 1:S + 1], ACT.Identity,
                                       scale=par[:, bass.ds(col, 1)],
                                       bias=par[:, bass.ds(col + 2 * 2 * FT, 1)]).then_inc(centre_ready, 1)

            up_chunk(0, True)
            with act.Fori(1, UPC) as c:
                up_chunk(c, False)
            split_at(G_DOWN + 3)
            act_high(UPC - 1)
            with act.Fori(0, DROW) as b:
                for j in range(4):
                    g = G_DOWN + 4 + j
                    split_hi(g % RAW, g % HIS, b * 16 + 16 * (g // RAW + 1), b * 4 + (g - HIS + 1))

            def out_square(cb, t):
                act.wait_ge(x2_ready, 2 * cb + t + 1)
                act.activation(junk3[:, t, :], res[:, t, 512 * cb:512 * cb + 512], ACT.Square,
                               accum_out=ssq3p[:, t, cb:cb + 1]).then_inc(squared, 1)

            act.preload_act_table(ACT.Sqrt)
            for n in range(4 * DROW + 4, 4 * DNB):
                split_at(G_DOWN + n)
                if (n - 4 * DROW - 4) % 3 == 1:
                    cb = (n - 4 * DROW - 4) // 3
                    if cb >= 1:
                        act.wait_ge(squared, T + 8 + 2 * cb)
                    for t in range(T):
                        out_square(cb, t)
            act.wait_ge(squared, T + 8 + 6)
            for t in range(T):
                out_square(3, t)
                act.wait_ge(stat_ready, 4 + 2 * t)
                act.activation(std3[:, t:t + 1], ssq3[:, t:t + 1], ACT.Sqrt, bias=eps[:, :], scale=1.0 / D)\
                    .then_inc(std_ready, 1)
                act.wait_ge(stat_ready, 5 + 2 * t)
                act.wait_ge(gained, 7 + t)
                for q in (2, 3):
                    cs = slice(512 * q, 512 * q + 512)
                    act.activation(yout[:, t, cs], yout[:, t, cs], ACT.Copy, scale=rs3[:, t:t + 1])\
                        .then_inc(y_ready[1], 1)

        @block.vector
        def _(dve):
            dve.memset(eps[:, :], EPS).then_inc(eps_ready, 1)
            def split_lo(slot_raw, slot_hi, ready):
                dve.wait_ge(hi_ready, ready)
                dve.tensor_tensor(wlo[:, slot_raw, :], raw[:, slot_raw, :], whi[:, slot_hi, :].bitcast(F32),
                                  ALU.subtract).then_inc(lo_ready, 1)

            def split_at(g):
                split_lo(g % RAW, g % HIS, g + 1)

            def turned_lo(dst, gain0, n0, tiles):
                for k in tiles:
                    dve.wait_ge(tile_hi, n0 + k + 2 - k % 2)
                    b, h = 4 + (k // 2) % 4, k % 2
                    dve.scalar_tensor_tensor(out=dst[:, k, S:2 * S], in0=ps[:, b, S * h:S * h + S],
                                             scalar=par[:, gain0 + k:gain0 + k + 1],
                                             in1=dst[:, k, 0:S].bitcast(F32), op0=ALU.mult,
                                             op1=ALU.subtract).then_inc(tile_lo, 1)

            def diagonal(dst, rs):
                for t in range(T):
                    ins = dve.tensor_scalar(dst[:, t, :], ident[:, :], rs[:, t:t + 1], None, ALU.mult)
                ins.then_inc(diag_ready, 1)

            dve.wait_ge(par_in_psum, 1)
            dve.tensor_copy(par[:, 0:CONV], ps[:, 0, 0:CONV]).then_inc(par_ready, 1)
            for g, n in enumerate(PIECES):
                for i in range(n):
                    last = i == n - 1
                    dve.wait_ge(hi_ready if last else piece_hi, g + 1 if last else pieces_before(g, i))
                    dve.tensor_tensor(wlo[:, g, piece(g, i)], raw[:, g, piece(g, i)],
                                      whi[:, g % HIS, piece(g, i)].bitcast(F32), ALU.subtract)\
                        .then_inc(lo_ready if last else piece_lo, 1)
                    if (g, i) == (0, 0):
                        turned_lo(xT, LN1, 0, range(4))
                    if g < 3 and i == n // 2:
                        turned_lo(xT, LN1, 0, range(4 * g + 4, 4 * g + 8))

            def rotary_tables():
                dve.wait_ge(rope_loaded, 64)
                for t in range(T):
                    for i in range(2):
                        dve.tensor_tensor(cosg[:, t, i, :], cosr[:, t, :], grow[:, i, :], ALU.mult)\
                            .then_inc(tables_ready, 1)
                        for e in range(2):
                            dve.tensor_tensor(sing[:, t, i, e::2], sinr[:, t, e::2], grow[:, i, 1 - e::2],
                                              ALU.mult).then_inc(tables_ready, 1)

            def over_heads(table, n):
                return table.unsqueeze(1).broadcast_to([P, n, table.shape[1]])

            groups = ((0, 0, GH), (1, GH, GKV))

            def rope(step, t):
                heads = gproj[:, t, 0:10 * DH].rearrange("p (h d) -> p h d", d=DH)
                base = 1 + 8 * t
                if step == "reciprocal":
                    dve.wait_ge(stdg_ready, 1)
                    dve.reciprocal(rsg, stdg).then_inc(rope_step, 1)
                if step == "scale":
                    dve.wait_ge(rope_step, base)
                    dve.tensor_tensor(rot_n[:, :, :], heads, rsg[:, t, :].unsqueeze(2).broadcast_to([P, 10, DH]),
                                      ALU.mult).then_inc(rope_step, 1)
                if step == "sines":
                    dve.wait_ge(tables_ready, 12)
                    dve.wait_ge(rope_step, base + 1)
                    for i, h0, n in groups:
                        for e in range(2):
                            dve.tensor_tensor(rot_m[:, h0:h0 + n, e::2], rot_n[:, h0:h0 + n, 1 - e::2],
                                              over_heads(sing[:, t, i, e::2], n), ALU.mult)\
                                .then_inc(rope_step, 1)
                if step == "cosines":
                    dve.wait_ge(rope_step, base + 5)
                    for i, h0, n in groups:
                        dve.tensor_tensor(rot_n[:, h0:h0 + n, :], rot_n[:, h0:h0 + n, :],
                                          over_heads(cosg[:, t, i, :], n), ALU.mult).then_inc(rope_step, 1)
                if step == "sum":
                    dve.wait_ge(rope_step, base + 7)
                    dve.tensor_tensor(heads, rot_n[:, :, :], rot_m[:, :, :], ALU.add).then_inc(rope_step, 1)

            ROPE = {16: [("reciprocal", 0), ("scale", 0)], 17: [("sines", 0)],
                    18: [("cosines", 0), ("sum", 0)], 19: [("scale", 1), ("sines", 1)],
                    20: [("cosines", 1)], 21: [("sum", 1)]}

            for g in range(len(PIECES), G_UP + 2):
                if g == 6:
                    dve.wait_ge(std_ready, 1)
                    dve.reciprocal(rs1, std1).then_inc(stat_ready, 1)
                    dve.wait_ge(stat_ready, 1)
                c = (g - 5) // 4
                if g == 6 or (g - 5) % 4 == 0 and 1 <= c < 5:
                    dve.wait_ge(granule_used, 4 * c + 4)
                    b = 2 * (c % 2)
                    dst = gproj[:, :, 512 * c:512 * c + 512] if c < 3 else \
                        nav[:, :, 512 * (c - 3):512 * (c - 3) + 512]
                    for t in range(T):
                        ins = dve.tensor_scalar(dst[:, t, :], ps[:, b + t, :], rs1[:, t:t + 1], None,
                                                ALU.mult)
                    ins.then_inc(banks_free, 1)
                c = (g - G_OUT - 3) // 2
                if (g - G_OUT - 3) % 2 == 0 and 0 <= c < 8:
                    dve.wait_ge(granule_used, g - 1)
                    dve.wait_ge(ors_ready, c // 4 + 1)
                    b = 2 * ((C_OUT + c) % 2)
                    cs = slice(512 * (c % 4), 512 * (c % 4) + 512)
                    if c >= 4:
                        dve.wait_ge(banks_free, C_OUT + c - 3)
                    for t in range(T):
                        ins = dve.scalar_tensor_tensor(out=res[:, t, cs], in0=ps[:, b + t, :],
                                                       scalar=rso[:, c // 4, t:t + 1], in1=res[:, t, cs],
                                                       op0=ALU.mult, op1=ALU.add)
                    ins.then_inc(banks_free, 1)
                if A_TURN + 2 <= g < A_TURN + 7:
                    i = g - A_TURN - 2
                    dve.wait_ge(g_hi, i + 1)
                    h0 = (2 * (i - 1)) % 10
                    dve.tensor_tensor(gT_lo[:, h0:h0 + 2, :], turned_heads,
                                      gT_hi[:, h0:h0 + 2, :].bitcast(F32), ALU.subtract).then_inc(g_lo, 1)
                a = g - A_SCORES - 2
                if 0 <= a < HEADS:
                    dve.wait_ge(scored, a + 1)
                    if a < GH:
                        dve.tensor_reduce(smax[:, a, :], scores_ps, AX.X, ALU.max).then_inc(max_ready, 1)
                        dve.wait_ge(max_ready, a + 1)
                        dve.tensor_scalar(nmax[:, a, :], smax[:, a, :], -SCALE, None, ALU.mult)\
                            .then_inc(nmax_ready, 1)
                    else:
                        n = a - GH
                        if n == 0:
                            dve.wait_ge(bias_masked, 4)
                        for t in range(T):
                            j0 = 2 - 2 * t
                            rev = bass.AP(bias, (n * 6 + j0) * GW + GW - 1,
                                          [[NAH * 6 * GW, P], [GW, ROWS], [-1, GW]])
                            dve.scalar_tensor_tensor(
                                out=biased[:, t, :].rearrange("p (r m) -> p r m", r=ROWS),
                                in0=scores_ps[:, t, :].rearrange("p (r m) -> p r m", r=ROWS),
                                scalar=SCALE, in1=rev, op0=ALU.mult, op1=ALU.add).then_inc(biased_ready, 1)
                        dve.wait_ge(biased_ready, 2 * n + 2)
                        dve.tensor_reduce(nmax[:, a, :], biased[:, :, :], AX.X, ALU.max, negate=True)\
                            .then_inc(nmax_ready, 1)

                split_at(g)

                if g == 6:
                    diagonal(diag1, rs1)
                if g == 7:
                    rotary_tables()
                if g == 8:
                    dve.wait_ge(par_in_psum, 2)
                    dve.tensor_copy(par[:, CONV:PARAMS], ps[:, 6, 0:PARAMS - CONV]).then_inc(par_ready, 1)
                c = (g - G_NAQK - 3) // 2
                if (g - G_NAQK - 3) % 2 == 0 and 0 <= c < 8:
                    dve.wait_ge(cross_copied, c + 1)
                    b = 2 * ((5 + c) % 2)
                    qk = naqkT[:, 2 * c:2 * c + 2, :]
                    dve.tensor_tensor(qk, ps[:, b:b + 2, 0:S], cross[:, :, :], ALU.add)\
                        .then_inc(banks_free, 1)
                    dve.wait_ge(banks_free, 6 + c)
                    dve.wait_ge(rms_ready, 1)
                    dve.tensor_tensor(qk, qk, over_heads(rms1[:, :], 2), ALU.mult).then_inc(qk_summed, 1)
                if g in NAQK_SPLIT:
                    pair = NAQK_SPLIT.index(g)
                    dve.wait_ge(qk_hi, pair + 1)
                    dve.tensor_tensor(naqk_lo[:, 4 * pair:4 * pair + 4, :], naqkT[:, 4 * pair:4 * pair + 4, :],
                                      naqk_hi[pair][:, :, :].bitcast(F32), ALU.subtract).then_inc(qk_lo, 1)
                for step, t in ROPE.get(g, ()):
                    rope(step, t)
                a = g - A_PV - 2
                if 0 <= a < HEADS:
                    dve.wait_ge(o_hi, a + 1)
                    tile = (a + NAH) % KT
                    dve.scalar_tensor_tensor(out=oT[:, tile, S:2 * S], in0=ps[:, 6, 0:S],
                                             scalar=par[:, NAG + tile:NAG + tile + 1],
                                             in1=oT[:, tile, 0:S].bitcast(F32), op0=ALU.mult,
                                             op1=ALU.subtract).then_inc(o_lo, 1)
                a = g - A_TRANSPOSE - 2
                if 0 <= a < HEADS:
                    dve.wait_ge(probT_hi_ready, a + 1)
                    dve.tensor_tensor(probT_lo[a // GH][:, a % 2], probT_ps, probT_hi[:, a % 2].bitcast(F32),
                                      ALU.subtract).then_inc(probT_lo_ready, 1)
                if g == 16:
                    dve.wait_ge(v_hi_ready, 1)
                    dve.tensor_tensor(gproj_r[:, :, GV:], gproj[:, :, GV:], gv_hi[:, :, :].bitcast(F32),
                                      ALU.subtract).then_inc(v_lo_ready, 1)
                if g in (28, 29):
                    t = g - 28
                    dve.wait_ge(v_hi_ready, 2 + t)
                    dve.tensor_tensor(nav_lo[:, t, :], nav[:, t, :], gproj_r[:, t, 0:NAH * DH].bitcast(F32),
                                      ALU.subtract).then_inc(v_lo_ready, 1)
                a = g - A_SCORES - 2
                if 0 <= a < HEADS:
                    dve.wait_ge(exp_done, 2 * a + 2)
                    dve.reciprocal(rsum[:, a, :], esum[:, a, :]).then_inc(rsum_ready, 1)
                    dve.wait_ge(rsum_ready, a + 1)
                    for t in range(T):
                        dve.tensor_scalar(prob[:, a % 2, t, :], prob[:, a % 2, t, :], rsum[:, a, t:t + 1],
                                          None, ALU.mult).then_inc(prob_ready, 1)
                for i, last in ((0, GH), (1, HEADS)):
                    if g == A_SUMSQ + last - 1 + 2:
                        dve.wait_ge(ostd_ready, i + 1)
                        dve.reciprocal(rso[:, i, :], stdo[:, i, :]).then_inc(ors_ready, 1)
                c = (g - G_OUT - 4) // 2
                if (g - G_OUT - 4) % 2 == 0 and 4 <= c < 7:
                    turned_lo(h2T, LN2, KT, range(4 * (c - 4), 4 * (c - 3)))
                if g == 46:
                    for e in (0, S + 1):
                        dve.memset(u[:, :, :, e:e + 1], 0.0).then_inc(pads_zero, 1)
            turned_lo(h2T, LN2, KT, range(12, 16))
            split_at(G_UP + 2)
            dve.wait_ge(squared, T + 8)
            dve.tensor_reduce(ssq2, ssq2p, AX.X, ALU.add).then_inc(stat_ready, 1)
            dve.wait_ge(std_ready, 2)
            dve.reciprocal(rs2, std2).then_inc(stat_ready, 1)
            dve.wait_ge(stat_ready, 3)
            diagonal(diag2, rs2)
            dve.wait_ge(pads_zero, 2)

            def act_low(c):
                dve.wait_ge(act_hi, c + 1)
                tiles = bass.ds(c * 2, 2)
                dve.tensor_tensor(actT[:, tiles, S:2 * S], prod[:, :, :],
                                  actT[:, tiles, 0:S].bitcast(F32), ALU.subtract).then_inc(act_lo, 1)

            def up_chunk(c, first):
                for j in range(4):
                    g = G_UP + 3 + j
                    split_lo(g % RAW, g % HIS, c * 4 + (g + 1))
                    half = j // 2
                    if j % 2 == 0:
                        b = 2 * ((C_UP + half) % 2)
                        dve.wait_ge(cross_copied, c * 2 + (8 + half + 1))
                        uc = u[:, half, :, 1:S + 1]
                        dve.tensor_tensor(uc, ps[:, b:b + 2, 0:S], cross[:, :, :], ALU.add)\
                            .then_inc(banks_free, 1)
                        dve.wait_ge(banks_free, c * 2 + (C_UP + half + 1))
                        if first and j == 0:
                            dve.wait_ge(rms_ready, 2)
                        dve.tensor_tensor(uc, uc, over_heads(rms2[:, :], 2), ALU.mult).then_inc(u_ready, 1)
                        if half == 0 and not first:
                            act_low(c - 1)
                        continue
                    dve.wait_ge(centre_ready, c * 4 + (2 * half + 2))
                    for f in range(2):
                        col = c * 2 + (CONV + half * FT + f)
                        dve.scalar_tensor_tensor(out=y[:, half, f, :], in0=u[:, half, f, 0:S],
                                                 scalar=par[:, bass.ds(col, 1)], in1=y[:, half, f, :],
                                                 op0=ALU.mult, op1=ALU.add).then_inc(tap_done, 1)
                    for f in range(2):
                        dve.wait_ge(tap_done, c * 4 + (2 * half + f + 1))
                        col = c * 2 + (CONV + 4 * FT + half * FT + f)
                        dve.scalar_tensor_tensor(out=y[:, half, f, :], in0=u[:, half, f, 2:S + 2],
                                                 scalar=par[:, bass.ds(col, 1)], in1=y[:, half, f, :],
                                                 op0=ALU.mult, op1=ALU.add).then_inc(conv_ready, 1)
                    if half == 1:
                        dve.wait_ge(silu_ready, c + 1)
                        dve.wait_ge(conv_ready, c * 4 + 4)
                        dve.tensor_tensor(prod[:, :, :], y[:, 0], y[:, 1], ALU.mult).then_inc(prod_ready, 1)

            up_chunk(0, True)
            with dve.Fori(1, UPC) as c:
                up_chunk(c, False)
            split_at(G_DOWN + 3)
            act_low(UPC - 1)
            with dve.Fori(0, DROW) as b:
                for j in range(4):
                    g = G_DOWN + 4 + j
                    split_lo(g % RAW, g % HIS, b * 4 + (g + 1))

            def add_ffn(cb, t):
                cs = slice(512 * cb, 512 * cb + 512)
                dve.tensor_tensor(res[:, t, cs], ps[:, (4 + 2 * cb + t) % 8, :], res[:, t, cs], ALU.add)\
                    .then_inc(x2_ready, 1)

            def gain(cb, t):
                cs = slice(512 * cb, 512 * cb + 512)
                dve.wait_ge(x2_ready, 2 * cb + t + 1)
                dve.tensor_tensor(yout[:, t, cs], res[:, t, cs], fgain[:, cs], ALU.mult).then_inc(gained, 1)

            dve.wait_ge(fgain_loaded, 16)
            for n in range(4 * DROW + 4, 4 * DNB):
                split_at(G_DOWN + n)
                if (n - 4 * DROW - 4) % 3 == 0:
                    cb = (n - 4 * DROW - 4) // 3
                    dve.wait_ge(granule_used, G_DOWN + n - 1)
                    for t in range(T):
                        add_ffn(cb, t)
                    for t in range(T):
                        gain(cb, t)
            for t in range(T):
                if t == 0:
                    dve.wait_ge(down_tile0, 1)
                else:
                    dve.wait_ge(granule_used, G_END)
                add_ffn(3, t)
                gain(3, t)
                dve.wait_ge(squared, T + 8 + 7 + t)
                dve.tensor_reduce(ssq3[:, t:t + 1], ssq3p[:, t, :], AX.X, ALU.add).then_inc(stat_ready, 1)
                dve.wait_ge(std_ready, 3 + t)
                dve.reciprocal(rs3[:, t:t + 1], std3[:, t:t + 1]).then_inc(stat_ready, 1)
                dve.wait_ge(stat_ready, 5 + 2 * t)
                dve.wait_ge(gained, 7 + t)
                for q in (0, 1):
                    cs = slice(512 * q, 512 * q + 512)
                    dve.tensor_scalar(yout[:, t, cs], yout[:, t, cs], rs3[:, t:t + 1], None, ALU.mult)\
                        .then_inc(y_ready[0], 1)

        @block.tensor
        def _(pe):
            def turn_tiles(n0, tiles):
                for k in tiles:
                    if k >= 8 and k % 2 == 0:
                        pe.wait_ge(tile_lo, n0 + k - 6)
                    b, h = 4 + (k // 2) % 4, k % 2
                    for t in range(T):
                        mm = pe.transpose(ps[:, b, S * h + P * t:S * h + P * t + P],
                                          res[:, t, P * k:P * k + P], ident[:, :])
                    mm.then_inc(tile_turned, 1)

            def spread(diag, n):
                pe.wait_ge(diag_ready, n)
                mm = pe.matmul(ps[:, 7, 0:S], ones[:, :], diag[:, :, :], start=True, stop=True)
                mm.then_inc(rms_spread, 1)

            def turn_column(cb):
                pe.wait_ge(banks_free, C_OUT + 4 + cb + 1)
                if cb == 0:
                    pe.wait_ge(ors_ready, 2)
                turn_tiles(KT, range(4 * cb, 4 * cb + 4))

            def tokens_granule(tok, k0, banks, raw_slot, hi_slot, first, last, tile0_done=None,
                               tiles=range(4)):
                hi = whi[:, hi_slot, :].rearrange("p (k n) -> p k n", k=4)
                lo = wlo[:, raw_slot, :].rearrange("p (k n) -> p k n", k=4)
                order = [(kk, t) for kk in tiles for t in range(T)]
                if tile0_done is not None:
                    order.sort(key=lambda kt: kt[1])
                for kk, t in order:
                    k, o = k0 + kk, ps[:, banks[t], :]
                    th, tl = tok[:, k, P * t:P * t + P], tok[:, k, S + P * t:S + P * t + P]
                    pe.matmul(o, th, hi[:, kk, :], start=first and kk == 0, stop=False)
                    pe.matmul(o, th, lo[:, kk, :], start=False, stop=False)
                    mm = pe.matmul(o, tl, hi[:, kk, :], start=False, stop=last and kk == 3)
                    if tile0_done is not None and (kk, t) == (3, 0):
                        mm.then_inc(tile0_done, 1)
                if 3 in tiles:
                    mm.then_inc(granule_used, 1)

            def weights_granule(tok, k0, banks, raw_slot, hi_slot, tiles=range(8)):
                hi = whi[:, hi_slot, :].rearrange("p (k n) -> p k n", k=8)
                lo = wlo[:, raw_slot, :].rearrange("p (k n) -> p k n", k=8)
                for f, b in enumerate(banks):
                    for kk in tiles:
                        k = k0 + kk
                        pe.matmul(ps[:, b, :], hi[:, kk, P * f:P * f + P], tok[:, k, :],
                                  start=k == 0, stop=False, skip_group_check=True)
                        mm = pe.matmul(ps[:, b, S:2 * S], lo[:, kk, P * f:P * f + P], tok[:, k, 0:S],
                                       start=False, stop=k == KT - 1, skip_group_check=True)
                if 7 in tiles:
                    mm.then_inc(granule_used, 1)

            def warm_up(n):
                for _ in range(n):
                    pe.matmul(ps[:, 3, 0:P], ones[:, :], ones[:, :], start=True, stop=True)

            pe.wait_ge(ones_ready, 1)
            warm_up(WARM1)
            pe.wait_ge(ident_ready, 1)
            pe.wait_ge(gains_loaded, 16)
            pe.transpose(ps[:, 0, 0:CONV], stage[0:CONV, 0, :], ident[0:CONV, 0:CONV])\
                .then_inc(par_in_psum, 1)

            def turn_quarter(h):
                pe.wait_ge(x_loaded[h], 16)
                turn_tiles(0, range(4 * h, 4 * h + 4))

            warm_up(WARM2)
            turn_quarter(0)
            for g, n in enumerate(PIECES):
                if g == 2:
                    turn_quarter(3)
                for i in range(n):
                    last = i == n - 1
                    pe.wait_ge(lo_ready if last else piece_lo, g + 1 if last else pieces_before(g, i))
                    tiles = range(4 // n * i, 4 // n * (i + 1))
                    pe.wait_ge(tile_lo, 4 * g + tiles[-1] + 1)
                    tokens_granule(xT, 4 * g, (0, 1), g, g % HIS, g == 0, g == 3, tiles=tiles)
                    if g < 2 and i == 0:
                        turn_quarter(g + 1)

            for g in range(len(PIECES), G_UP):
                pe.wait_ge(lo_ready, g + 1)
                if g < G_NAQK:
                    chunk, kq = divmod(g, 4)
                    if kq == 0 and chunk >= 2:
                        pe.wait_ge(banks_free, chunk - 1)
                    b = 2 * (chunk % 2)
                    tokens_granule(xT, 4 * kq, (b, b + 1), g % RAW, g % HIS, kq == 0, kq == 3)
                elif g < G_OUT:
                    c, kh = divmod(g - G_NAQK, 2)
                    chunk = 5 + c
                    if kh == 0:
                        pe.wait_ge(banks_free, chunk - 1)
                    b = 2 * (chunk % 2)
                    weights_granule(xT, 8 * kh, (b, b + 1), g % RAW, g % HIS)
                else:
                    c, kh = divmod(g - G_OUT, 2)
                    chunk = C_OUT + c
                    if kh == 0:
                        pe.wait_ge(banks_free, chunk - 1)
                    if c in (0, 4):
                        pe.wait_ge(o_lo, GH if c == 0 else HEADS)
                    b = 2 * (chunk % 2)
                    tokens_granule(oT, (NAH if c < 4 else 0) + 4 * kh, (b, b + 1), g % RAW, g % HIS,
                                   kh == 0, kh == 1)

                if g == 6:
                    pe.wait_ge(conv_loaded, 16)
                    for j in range(4):
                        mm = pe.transpose(ps[:, 6, 2 * FT * j:2 * FT * (j + 1)], stage[0:2 * FT, 1 + j, :],
                                          ident[0:2 * FT, 0:2 * FT])
                    mm.then_inc(par_in_psum, 1)
                if g == 8:
                    pe.wait_ge(ones_ready, 1)
                    spread(diag1, 1)
                if A_TURN <= g < A_TURN + 5:
                    i = g - A_TURN
                    if i == 0:
                        pe.wait_ge(rope_step, 17)
                    else:
                        pe.wait_ge(g_lo, i)
                    h0 = (2 * (i - 1)) % 10
                    for h in range(2):
                        for t in range(T):
                            mm = pe.transpose(ps[:, 7, S * h + P * t:S * h + P * t + P],
                                              gproj[:, t, DH * (h0 + h):DH * (h0 + h) + DH], ident[:, :])
                    mm.then_inc(g_turned, 1)
                a = g - A_SCORES
                if 0 <= a < HEADS:
                    if a < GH:
                        pe.wait_ge(g_lo, 2 + a // 2)
                        kv = GH + a // (GH // GKV)
                        qh, ql, kh, kl = gT_hi[:, a, :], gT_lo[:, a, :], gT_hi[:, kv, :], gT_lo[:, kv, :]
                    else:
                        pair, i = divmod(a - GH, 2)
                        pe.wait_ge(qk_lo, pair + 1)
                        qh, kh = naqk_hi[pair][:, i, :], naqk_hi[pair][:, 2 + i, :]
                        ql, kl = naqk_lo[:, 4 * pair + i, :], naqk_lo[:, 4 * pair + 2 + i, :]
                    if a >= 1:
                        pe.wait_ge(exp_done, 2 * a)
                    for t in range(T):
                        o, rows = scores_ps[:, t, :], slice(P * t, P * t + P)
                        pe.matmul(o, qh[:, rows], kh, start=True, stop=False)
                        pe.matmul(o, qh[:, rows], kl, start=False, stop=False)
                        mm = pe.matmul(o, ql[:, rows], kh, start=False, stop=True)
                    mm.then_inc(scored, 1)
                a = g - A_TRANSPOSE
                if 0 <= a < HEADS:
                    pe.wait_ge(prob_ready, 2 * a + 2)
                    if a >= 1:
                        pe.wait_ge(probT_lo_ready, a)
                    for k in range(T):
                        for t in range(T):
                            mm = pe.transpose(probT_ps[:, k, P * t:P * t + P],
                                              prob[:, a % 2, t, P * k:P * k + P], ident[:, :])
                    mm.then_inc(prob_turned, 1)
                a = g - A_PV
                if 0 <= a < HEADS:
                    pe.wait_ge(probT_lo_ready, a + 1)
                    pe.wait_ge(v_lo_ready, 1 if a < GH else 3)
                    if a == 0:
                        pe.wait_ge(par_ready, 2)
                    else:
                        pe.wait_ge(o_lo, a)
                    for k in range(T):
                        if a < GH:
                            v0 = a // (GH // GKV) * DH
                            vh, vl = gv_hi[:, k, v0:v0 + DH], gproj_r[:, k, GV + v0:GV + v0 + DH]
                        else:
                            cs = slice(DH * (a - GH), DH * (a - GH) + DH)
                            vh, vl = gproj_r[:, k, cs], nav_lo[:, k, cs]
                        ph, pl = probT_hi[:, a % 2, k, :], probT_lo[a // GH][:, a % 2, k, :]
                        o = ps[:, 6, 0:S]
                        pe.matmul(o, vh, ph, start=k == 0, stop=False)
                        pe.matmul(o, vh, pl, start=False, stop=False)
                        mm = pe.matmul(o, vl, ph, start=False, stop=k == T - 1)
                    mm.then_inc(pv_done, 1)
                for i, last in ((0, GH), (1, HEADS)):
                    if g == A_SUMSQ + last - 1:
                        pe.wait_ge(osq_summed, last)
                        pe.wait_ge(g_lo, 5)
                        if i == 1:
                            pe.wait_ge(ostd_ready, 1)
                        for t in range(T):
                            mm = pe.matmul(headsq_ps[:, i, t:t + 1], osum[:, i, P * t:P * t + P],
                                           ones[:, 0:1], start=True, stop=True)
                        mm.then_inc(group_summed, 1)
                c = (g - G_OUT - 10) / 2
                if c in (0, 1, 2):
                    turn_column(int(c))

            def up_granule(c, j, tiles=range(8)):
                g = G_UP + j
                pe.wait_ge(lo_ready, c * 4 + (g + 1))
                chunk = C_UP + j // 2
                if j % 2 == 0:
                    pe.wait_ge(banks_free, c * 2 + (chunk - 1))
                b = 2 * (chunk % 2)
                weights_granule(h2T, 8 * (j % 2), (b, b + 1), g % RAW, g % HIS, tiles)

            pe.wait_ge(tile_lo, KT + 12)
            up_granule(0, 0)
            turn_column(3)
            up_granule(0, 1, range(4))
            pe.wait_ge(tile_lo, 2 * KT)
            up_granule(0, 1, range(4, 8))
            up_granule(0, 2)
            spread(diag2, 2)
            up_granule(0, 3)
            with pe.Fori(1, UPC) as c:
                for j in range(4):
                    up_granule(c, j)

            for n, (blk, cb) in enumerate(DOWN):
                g = G_DOWN + n
                pe.wait_ge(lo_ready, g + 1)
                if cb == 0:
                    pe.wait_ge(act_lo, 2 * blk + 2)
                if n == 2:
                    pe.wait_ge(banks_free, C_UP + 2 * UPC)
                b = (4 + 2 * cb) % 8
                tokens_granule(actT, 4 * blk, (b, b + 1), g % RAW, g % HIS, blk == 0, blk == DNB - 1,
                               tile0_done=down_tile0 if g == G_END - 1 else None)


_INS = ["x", "w_in", "na_rpb", "q_norm_g", "k_norm_g", "w_out", "w_up", "w_down", "final_g"]


def kernel(**inputs):
    import numpy as _np
    import concourse.bacc as _bacc
    from concourse import mybir as _mybir
    from concourse.bass_utils import run_bass_kernel_spmd as _run

    nc = _bacc.Bacc("TRN2", target_bir_lowering=False, num_devices=1)
    arrays, args = {}, []

    def give(name, a):
        arrays[f"in_{name}_dram"] = a
        args.append(nc.dram_tensor(f"in_{name}_dram", a.shape, _mybir.dt.from_np(a.dtype),
                                   kind="ExternalInput").ap())

    for name in _INS:
        a = _np.asarray(inputs[name])
        if name == "na_rpb":
            a = a[..., ::-1]
        give(name, _np.ascontiguousarray(a))
    rows = lambda name: _np.asarray(inputs[name]).reshape(-1, P)
    give("gains", _np.concatenate([rows(n) for n in ("ln1_g", "ln2_g", "na_out_g", "gqa_out_g")]))
    give("conv", _np.concatenate([_np.asarray(inputs["conv_w"])[0], _np.asarray(inputs["conv_b"])]))
    t = _np.arange(S)
    inv = (1.0 / (10000.0 ** (_np.arange(0, DH // 2, 2, dtype=_np.float32) / (DH // 2)))).astype(_np.float32)
    ang = _np.concatenate([(t // GW).astype(_np.float32)[:, None] * inv,
                           (t % GW).astype(_np.float32)[:, None] * inv], axis=-1)
    give("cos", _np.repeat(_np.cos(ang), 2, axis=-1).astype(_np.float32))
    give("sin", _np.stack([-_np.sin(ang), _np.sin(ang)], axis=-1).reshape(S, DH).astype(_np.float32))
    args.append(nc.dram_tensor("out_0_dram", (1, S, D), F32, kind="ExternalOutput").ap())
    hybrid_block(nc, *args)
    r = _run(nc, [arrays], core_ids=[0])
    return r.results[0]["out_0_dram"]
```
